# Optimizing a Trainium2 kernel written in Bass

```python
import math
import jax, jax.numpy as jnp
from jax import lax
import numpy as np

D_MODEL = 1024
BATCH = 1
SEQ = 2048
DEPTH = 1

CHUNK = 64
Q_BLOCK = 128

MLA_HEADS = 8
MLA_NOPE = 64
MLA_ROPE = 32
MLA_V = 64
MLA_Q_RANK = 256
MLA_KV_RANK = 128
ROPE_THETA = 10000.0
D_MLA = MLA_HEADS * MLA_V

HG_HEADS = 4
HG_DK = 128
HG_DV = 128
D_HG = HG_HEADS * HG_DV

D_MIX = D_MLA + D_HG
IN_SIZES = (MLA_Q_RANK, MLA_KV_RANK, MLA_ROPE, HG_HEADS * HG_DK, HG_HEADS * HG_DV, HG_HEADS * HG_DK, HG_HEADS * HG_DV)
IN_COLS = sum(IN_SIZES)

N_GROUPS = 4
EXPERTS_PER_GROUP = 8
N_EXPERTS = N_GROUPS * EXPERTS_PER_GROUP
TOP_K = 2
D_EXPERT = 512
MOE_BLOCK = 128

RMS_EPS = 1e-6
LN_EPS = 1e-5
ALPHA = (2.0 * DEPTH) ** 0.25
BETA = (8.0 * DEPTH) ** -0.25

kernel_name = "hybrid_mla_hgrn2_hiermoe_deepnorm"

def rms_norm(x, g):
    xf = x.astype(jnp.float32)
    y = xf * lax.rsqrt(jnp.mean(xf * xf, axis=-1, keepdims=True) + RMS_EPS)
    return (y * g.astype(jnp.float32)).astype(x.dtype)

def layer_norm(x, g, b):
    xf = x.astype(jnp.float32)
    mu = jnp.mean(xf, axis=-1, keepdims=True)
    xc = xf - mu
    var = jnp.mean(xc * xc, axis=-1, keepdims=True)
    y = xc * lax.rsqrt(var + LN_EPS) * g.astype(jnp.float32) + b.astype(jnp.float32)
    return y.astype(x.dtype)

def rope(x, cos, sin):
    x1, x2 = jnp.split(x, 2, axis=-1)
    return jnp.concatenate([x1 * cos - x2 * sin, x2 * cos + x1 * sin], axis=-1)

def mla_group(c_q, c_kv, k_r, positions, q_norm_g, w_uq, kv_norm_g, w_ukv):
    B, S, _ = c_q.shape
    dt = c_q.dtype
    inv_freq = ROPE_THETA ** (-jnp.arange(0, MLA_ROPE, 2, dtype=jnp.float32) / MLA_ROPE)
    ang = positions.astype(jnp.float32)[..., None] * inv_freq
    cos = jnp.cos(ang).astype(dt)
    sin = jnp.sin(ang).astype(dt)
    q = (rms_norm(c_q, q_norm_g) @ w_uq).reshape(B, S, MLA_HEADS, MLA_NOPE + MLA_ROPE)
    q_nope = q[..., :MLA_NOPE]
    q_rope = rope(q[..., MLA_NOPE:], cos[:, :, None, :], sin[:, :, None, :])
    kv = (rms_norm(c_kv, kv_norm_g) @ w_ukv).reshape(B, S, MLA_HEADS, MLA_NOPE + MLA_V)
    k_nope = kv[..., :MLA_NOPE]
    v = kv[..., MLA_NOPE:]
    k_rope = rope(k_r, cos, sin)
    scale = (MLA_NOPE + MLA_ROPE) ** -0.5
    nqb = S // Q_BLOCK
    key_chunk = jnp.arange(S, dtype=jnp.int32) // CHUNK

    def one_block(args):
        qn, qr, qb = args
        s = jnp.einsum('bqhd,bkhd->bhqk', qn, k_nope) + jnp.einsum('bqhr,bkr->bhqk', qr, k_rope)
        s = s.astype(jnp.float32) * scale
        q_chunk = (qb * Q_BLOCK + jnp.arange(Q_BLOCK, dtype=jnp.int32)) // CHUNK
        mask = key_chunk[None, :] <= q_chunk[:, None]
        p = jax.nn.softmax(jnp.where(mask, s, -jnp.inf), axis=-1).astype(v.dtype)
        return jnp.einsum('bhqk,bkhd->bqhd', p, v)

    qn_b = q_nope.reshape(B, nqb, Q_BLOCK, MLA_HEADS, MLA_NOPE).transpose(1, 0, 2, 3, 4)
    qr_b = q_rope.reshape(B, nqb, Q_BLOCK, MLA_HEADS, MLA_ROPE).transpose(1, 0, 2, 3, 4)
    out = lax.map(one_block, (qn_b, qr_b, jnp.arange(nqb, dtype=jnp.int32)))
    return out.transpose(1, 0, 2, 3, 4).reshape(B, S, D_MLA)

def hgrn2_group(f_pre, i_in, q_in, g_in, lb_logits, layer, hg_norm_g):
    B, S, _ = f_pre.shape
    dt = f_pre.dtype
    lb = jnp.cumsum(jax.nn.softmax(lb_logits.astype(jnp.float32), axis=0), axis=0)[layer]
    f = lb + (1.0 - lb) * jax.nn.sigmoid(f_pre.astype(jnp.float32))
    log_f = jnp.log(f)
    k = 1.0 - f
    nc = S // CHUNK

    def to_chunks(t, d):
        return t.astype(jnp.float32).reshape(B, nc, CHUNK, HG_HEADS, d).transpose(1, 0, 3, 2, 4)

    qc = to_chunks(q_in, HG_DK)
    kc = to_chunks(k, HG_DK)
    vc = to_chunks(i_in, HG_DV)
    lfc = to_chunks(log_f, HG_DK)
    causal = jnp.tril(jnp.ones((CHUNK, CHUNK), dtype=bool))

    def step(state, inp):
        q, kk, v, lf = inp
        b = jnp.cumsum(lf, axis=2)
        diff = b[:, :, :, None, :] - b[:, :, None, :, :]
        decay = jnp.exp(jnp.where(causal[:, :, None], diff, -jnp.inf))
        a = jnp.einsum('bhtd,bhsd,bhtsd->bhts', q, kk, decay)
        o = jnp.einsum('bhts,bhse->bhte', a, v) + jnp.einsum('bhtd,bhde->bhte', q * jnp.exp(b), state)
        b_last = b[:, :, -1:, :]
        new_state = jnp.exp(b_last[:, :, 0, :])[..., None] * state + jnp.einsum('bhsd,bhse->bhde', kk * jnp.exp(b_last - b), v)
        return new_state, o

    s0 = jnp.zeros((B, HG_HEADS, HG_DK, HG_DV), jnp.float32)
    _, o = lax.scan(step, s0, (qc, kc, vc, lfc))
    o = o.transpose(1, 0, 3, 2, 4).reshape(B, S, HG_HEADS, HG_DV)
    g = g_in.astype(jnp.float32).reshape(B, S, HG_HEADS, HG_DV)
    o = rms_norm(o, hg_norm_g) * jax.nn.silu(g)
    return o.reshape(B, S, D_HG).astype(dt)

def hier_moe(h, w_router_group, b_router_group, w_router_expert, b_router_expert, w1, w3, w2):
    B, S, D = h.shape
    N = B * S
    xt = h.reshape(N, D)
    g_logits = (xt @ w_router_group).astype(jnp.float32) + b_router_group.astype(jnp.float32)
    g_prob = jax.nn.softmax(g_logits, axis=-1)
    grp = jnp.argmax(g_logits, axis=-1).astype(jnp.int32)
    p_grp = jnp.take_along_axis(g_prob, grp[:, None], axis=-1)
    e_logits = ((xt @ w_router_expert).astype(jnp.float32) + b_router_expert.astype(jnp.float32)).reshape(N, N_GROUPS, EXPERTS_PER_GROUP)
    e_in = jnp.take_along_axis(e_logits, grp[:, None, None], axis=1)[:, 0]
    top_v, top_i = lax.top_k(e_in, TOP_K)
    gate = p_grp * jax.nn.softmax(top_v, axis=-1)
    expert = grp[:, None] * EXPERTS_PER_GROUP + top_i.astype(jnp.int32)

    A = N * TOP_K
    eid = expert.reshape(A)
    tid = jnp.repeat(jnp.arange(N, dtype=jnp.int32), TOP_K)
    gflat = gate.reshape(A)
    counts = jnp.zeros((N_EXPERTS,), jnp.int32).at[eid].add(1)
    padded = ((counts + MOE_BLOCK - 1) // MOE_BLOCK) * MOE_BLOCK
    pad_end = jnp.cumsum(padded)
    pad_start = pad_end - padded
    raw_start = jnp.cumsum(counts) - counts
    order = jnp.argsort(eid)
    se = eid[order]
    dest = pad_start[se] + (jnp.arange(A, dtype=jnp.int32) - raw_start[se])
    nb = (A + N_EXPERTS * (MOE_BLOCK - 1) + MOE_BLOCK - 1) // MOE_BLOCK
    P = nb * MOE_BLOCK
    slot_tok = jnp.full((P,), N, jnp.int32).at[dest].set(tid[order])
    slot_gate = jnp.zeros((P,), jnp.float32).at[dest].set(gflat[order])
    block_start = jnp.arange(nb, dtype=jnp.int32) * MOE_BLOCK
    block_exp = jnp.minimum(jnp.searchsorted(pad_end, block_start, side='right'), N_EXPERTS - 1).astype(jnp.int32)
    x_pad = jnp.concatenate([xt, jnp.zeros((1, D), xt.dtype)], axis=0)
    xb = x_pad[slot_tok].reshape(nb, MOE_BLOCK, D)

    def run_block(args):
        xblk, e = args
        return (jax.nn.silu(xblk @ w1[e]) * (xblk @ w3[e])) @ w2[e]

    yb = lax.map(run_block, (xb, block_exp)).reshape(P, D)
    out = jnp.zeros((N + 1, D), yb.dtype).at[slot_tok].add(yb * slot_gate[:, None].astype(yb.dtype))
    return out[:N].reshape(B, S, D)

def setup_inputs(seed: int = 0) -> dict:
    key = jax.random.key(seed)
    ks = jax.random.split(key, 24)

    def nrm(k, shape, scale):
        return jax.random.normal(k, shape, jnp.float32) * scale

    x = nrm(ks[0], (BATCH, SEQ, D_MODEL), 1.0)
    positions = jax.random.randint(ks[1], (BATCH, 1), 0, 65536, dtype=jnp.int32) + jnp.arange(SEQ, dtype=jnp.int32)[None, :]
    col_scale = jnp.concatenate([
        jnp.ones((MLA_Q_RANK + MLA_KV_RANK + MLA_ROPE + HG_HEADS * HG_DK,), jnp.float32),
        jnp.full((HG_HEADS * HG_DV,), BETA, jnp.float32),
        jnp.ones((HG_HEADS * HG_DK + HG_HEADS * HG_DV,), jnp.float32)])
    w_in = nrm(ks[2], (DEPTH, D_MODEL, IN_COLS), D_MODEL ** -0.5) * col_scale
    q_norm_g = 1.0 + nrm(ks[3], (DEPTH, MLA_Q_RANK), 0.02)
    w_uq = nrm(ks[4], (DEPTH, MLA_Q_RANK, MLA_HEADS * (MLA_NOPE + MLA_ROPE)), MLA_Q_RANK ** -0.5)
    kv_norm_g = 1.0 + nrm(ks[5], (DEPTH, MLA_KV_RANK), 0.02)
    kv_scale = jnp.concatenate([jnp.ones((MLA_NOPE,), jnp.float32), jnp.full((MLA_V,), BETA, jnp.float32)])
    w_ukv = (nrm(ks[6], (DEPTH, MLA_KV_RANK, MLA_HEADS, MLA_NOPE + MLA_V), MLA_KV_RANK ** -0.5) * kv_scale).reshape(DEPTH, MLA_KV_RANK, MLA_HEADS * (MLA_NOPE + MLA_V))
    mla_out_g = 1.0 + nrm(ks[7], (DEPTH, D_MLA), 0.02)
    hg_lb_logits = nrm(ks[8], (DEPTH + 1, HG_HEADS * HG_DK), 0.5)
    hg_norm_g = 1.0 + nrm(ks[9], (DEPTH, HG_DV), 0.02)
    w_out = nrm(ks[10], (DEPTH, D_MIX, D_MODEL), D_MIX ** -0.5 * BETA)
    ln1_g = 1.0 + nrm(ks[11], (DEPTH, D_MODEL), 0.02)
    ln1_b = nrm(ks[12], (DEPTH, D_MODEL), 0.02)
    w_router_group = nrm(ks[13], (DEPTH, D_MODEL, N_GROUPS), D_MODEL ** -0.5)
    b_router_group = nrm(ks[14], (DEPTH, N_GROUPS), 0.01)
    w_router_expert = nrm(ks[15], (DEPTH, D_MODEL, N_EXPERTS), D_MODEL ** -0.5)
    b_router_expert = nrm(ks[16], (DEPTH, N_EXPERTS), 0.01)
    w1 = nrm(ks[17], (DEPTH, N_EXPERTS, D_MODEL, D_EXPERT), D_MODEL ** -0.5 * BETA)
    w3 = nrm(ks[18], (DEPTH, N_EXPERTS, D_MODEL, D_EXPERT), D_MODEL ** -0.5 * BETA)
    w2 = nrm(ks[19], (DEPTH, N_EXPERTS, D_EXPERT, D_MODEL), D_EXPERT ** -0.5 * BETA)
    ln2_g = 1.0 + nrm(ks[20], (DEPTH, D_MODEL), 0.02)
    ln2_b = nrm(ks[21], (DEPTH, D_MODEL), 0.02)
    return {"x": x, "positions": positions, "w_in": w_in, "q_norm_g": q_norm_g, "w_uq": w_uq,
            "kv_norm_g": kv_norm_g, "w_ukv": w_ukv, "mla_out_g": mla_out_g, "hg_lb_logits": hg_lb_logits,
            "hg_norm_g": hg_norm_g, "w_out": w_out, "ln1_g": ln1_g, "ln1_b": ln1_b,
            "w_router_group": w_router_group, "b_router_group": b_router_group,
            "w_router_expert": w_router_expert, "b_router_expert": b_router_expert,
            "w1": w1, "w3": w3, "w2": w2, "ln2_g": ln2_g, "ln2_b": ln2_b}

def reference(x, positions, w_in, q_norm_g, w_uq, kv_norm_g, w_ukv, mla_out_g, hg_lb_logits, hg_norm_g,
              w_out, ln1_g, ln1_b, w_router_group, b_router_group, w_router_expert, b_router_expert,
              w1, w3, w2, ln2_g, ln2_b):
    split_idx = [int(v) for v in np.cumsum(IN_SIZES)[:-1]]
    h = x
    for l in range(DEPTH):
        proj = h @ w_in[l]
        c_q, c_kv, k_r, f_pre, i_in, q_in, g_in = jnp.split(proj, split_idx, axis=-1)
        a = rms_norm(mla_group(c_q, c_kv, k_r, positions, q_norm_g[l], w_uq[l], kv_norm_g[l], w_ukv[l]), mla_out_g[l])
        r = hgrn2_group(f_pre, i_in, q_in, g_in, hg_lb_logits, l, hg_norm_g[l])
        mix = jnp.concatenate([a, r], axis=-1) @ w_out[l]
        h = layer_norm(ALPHA * h + mix, ln1_g[l], ln1_b[l])
        moe = hier_moe(h, w_router_group[l], b_router_group[l], w_router_expert[l], b_router_expert[l], w1[l], w3[l], w2[l])
        h = layer_norm(ALPHA * h + moe, ln2_g[l], ln2_b[l])
    return h


_drawn_inputs = setup_inputs


def setup_inputs(seed=0):
    import zlib

    import numpy as np

    out = dict(_drawn_inputs(seed))
    spreads = {}
    factors = {'q_norm_g': 8.0,
     'kv_norm_g': 4.139,
     'mla_out_g': 7.863,
     'hg_norm_g': 24.769,
     'ln1_g': 2.752,
     'ln1_b': 2.792,
     'b_router_group': 23.076,
     'b_router_expert': 23.907,
     'ln2_g': 8.752,
     'ln2_b': 8.125}
    for name, (base, spread) in spreads.items():
        noise = np.random.default_rng([zlib.crc32(name.encode()), seed]).standard_normal(out[name].shape)
        drawn = base * np.exp(spread * noise) if base else spread * noise
        out[name] = __import__('jax').numpy.asarray(drawn.astype(out[name].dtype))
    for name, factor in factors.items():
        out[name] = (out[name] * factor).astype(out[name].dtype)
    return out
```

```python
from contextlib import ExitStack

import numpy as np
import concourse.bass as bass
from concourse import mybir

F32 = mybir.dt.float32
I32 = mybir.dt.int32
U32 = mybir.dt.uint32
F32R = mybir.dt.float32r
ALU = mybir.AluOpType
ACT = mybir.ActivationFunctionType
AX = mybir.AxisListType.X

P = 128
SEQ, DM = 2048, 1024
KT = DM // P
Q_RANK, KV_RANK, ROPE = 256, 128, 32
NOPE, VD, HEADS = 64, 64, 8
HG, DK = 4, 128
D_HG = HG * DK
NG, EPG = 4, 8
NE = NG * EPG
DE = 512
NT = SEQ // P
ALPHA = 2.0 ** 0.25
RMS_EPS, LN_EPS = 1e-6, 1e-5
SCALE = (NOPE + ROPE) ** -0.5
NB = (SEQ * 2 + NE * (P - 1)) // P
NBP = NB + 1

SPAN = 256
NS = SEQ // SPAN
C = 32
NC = SPAN // C

W_CQ, W_CKV, W_KR, W_F = 0, 256, 384, 448
W_I, W_Q, W_G = W_F + 512, W_F + 1024, W_F + 1536
W_COLS = W_F + 2048

C_INVF, C_TURN, C_RAD, C_SIGN, C_REPS, C_LEPS = range(6)

R_EXPERT, R_GROUP, R_BLOCK = 0, NE, 2 * NE
BIG = 3.0e38

PI2_A = 6.28125
PI2_B = float(np.float32(round((2 * np.pi - PI2_A) * 2.0 ** 21) / 2.0 ** 21))
PI2_C = float(np.float32(2 * np.pi - PI2_A - PI2_B))
ROUND = 12582912.0


class Hold:

    def __init__(self, op, cell, sem):
        self.op, self.cell, self.sem = op, cell, sem

    def __call__(self, eng, before):
        eng.wait_ge(self.sem, before)
        if self.op == "memset":
            ins = eng.memset(self.cell[:, 0:1], 0.0)
        else:
            ins = eng.tensor_tensor(self.cell[:, 3:4], self.cell[:, 4:5], self.cell[:, 4:5], ALU.add)
        ins.then_inc(self.sem, 1)


def shape_constants():
    c = {}
    c["ident"] = np.eye(P, dtype=np.float32)
    s = np.arange(P)
    c["causal"] = ((s[:, None] <= s[None, :]) & (s[:, None] // C == s[None, :] // C)).astype(np.float32)
    c["before"] = (s[:, None] < s[None, :]).astype(np.float32)
    col = np.zeros((P, 8), np.float32)
    freq = (np.float32(10000.0) ** (-(np.arange(0, ROPE, 2, dtype=np.float32) / np.float32(ROPE)))).astype(np.float32)
    j = s % 64
    col[:, C_INVF] = freq[j % 16]
    col[:, C_TURN] = np.where(j < 32, 0.25, 0.0)
    col[:, C_RAD] = np.where(j < 32, np.pi / 2, 0.0)
    col[:, C_SIGN] = np.where((j >= 32) & (j < 48), -1.0, 1.0)
    col[:, C_REPS] = RMS_EPS
    col[:, C_LEPS] = LN_EPS
    c["cols"] = col
    fold = np.zeros((P, P), np.float32)
    fold[:64, 64:] = (s[:64, None] % 32 == s[None, :64] % 32)
    c["fold"] = fold
    c["restart_tiles"] = np.tile((np.arange(NT * NE) % NT != 0).astype(np.float32), (P, 1))
    row = np.zeros((P, 2 * NE + NBP), np.float32)
    row[:, R_EXPERT:R_EXPERT + NE] = np.arange(NE)
    row[:, R_GROUP:R_GROUP + NE] = np.arange(NE) // EPG
    row[:, R_BLOCK:R_BLOCK + NBP] = np.arange(NBP)
    c["rows"] = row
    c["token"] = (np.arange(NT)[None, :] * P + s[:, None]).astype(np.int32)
    c["restart"] = np.tile((np.arange(HG * SPAN) % C != 0).astype(np.float32), (P, 1))
    return c


def lay_out(inputs):
    a = {n: np.asarray(v) for n, v in inputs.items()}
    cols = np.concatenate([np.arange(416), np.arange(400, 416), np.arange(384, 400), np.arange(416, 2464)])
    column = lambda v: np.ascontiguousarray(v.reshape(-1, P).T)
    a["w_in"] = np.ascontiguousarray(a["w_in"][0][:, cols])
    for n in ("q_norm_g", "kv_norm_g", "hg_norm_g"):
        a[n] = column(a[n][0])
    a["mla_out_g"] = column(a["mla_out_g"][0])
    a["w_router"] = np.concatenate([a["w_router_group"][0], a["w_router_expert"][0]], axis=1)
    a["b_router"] = np.concatenate([a["b_router_group"], a["b_router_expert"]], axis=1)
    w = a["w_uq"][0].reshape(Q_RANK, HEADS, NOPE + ROPE)
    w = w[:, :, np.concatenate([np.arange(96), np.arange(80, 96), np.arange(64, 80)])]
    a["w_uq"] = np.ascontiguousarray(w.reshape(Q_RANK, HEADS // 2, 2, P).transpose(1, 0, 2, 3))
    w = a["w_ukv"][0].reshape(KV_RANK, HEADS // 2, 2, 2, NOPE)
    a["w_ukv"] = np.ascontiguousarray(w.transpose(1, 3, 0, 2, 4))
    a["hg_lb_logits"] = np.ascontiguousarray(a["hg_lb_logits"].reshape(2, HG, P).transpose(2, 0, 1))
    return a


def phase_0(nc, t, d):
    with ExitStack() as ctx:
        sb = lambda name, shape, dt=F32: ctx.enter_context(nc.sbuf_tensor(name, shape, dt))
        sem = lambda name: ctx.enter_context(nc.semaphore(name))
        pos_i = sb("pos_i", [P, SEQ], I32)
        ang = sb("ang", [P, SEQ])
        turns = sb("turns", [P, SEQ])
        lbl = sb("lbl", [P, 2, HG])
        lbm = sb("lbm", [P, HG])
        lbe = sb("lbe", [P, 2, HG])
        lbs = sb("lbs", [P, HG])
        loaded = sem("const_loaded")
        steps = sem("dve0_steps")
        act_steps = sem("act0_steps")
        with nc.Block() as block:
            @block.sync
            def _(sp):
                for dst, src in (
                    (t["ident"][:], d["ident"]), (t["causal"][:], d["causal"]), (t["fold"][:], d["fold"]),
                    (t["cols"][:], d["cols"]), (t["restart"][:], d["restart"]),
                    (pos_i[:], d["positions"].broadcast_to([P, SEQ])),
                    (lbl[:], d["hg_lb_logits"]), (t["gq"][:], d["q_norm_g"]),
                    (t["gkv"][:], d["kv_norm_g"]), (t["ghg"][:], d["hg_norm_g"]),
                ):
                    sp.dma_start(dst, src).then_inc(loaded, 16)
                w = d["w_in"].rearrange("(k p) n -> p k n", p=P)
                for k in range(KT):
                    sp.dma_start(t["wi"][:, k], w[:, k]).then_inc(t["w_in_loaded"], 16)
                sp.wait_ge(loaded, 160)

            @block.scalar
            def _(act):
                act.wait_ge(steps, 6)
                nc.scalar.activation(lbe[:], lbl[:], ACT.Exp).then_inc(act_steps, 1)
                act.wait_ge(steps, 15)
                nc.scalar.activation(t["trig"][:], ang[:], ACT.Sin).then_inc(act_steps, 1)

            @block.vector
            def _(v):
                n = [0]

                def step(ins, after=True):
                    n[0] += 1
                    ins.then_inc(steps, 1)
                    v.wait_ge(steps, n[0])
                v.wait_ge(loaded, 160)
                step(v.tensor_copy(ang[:], pos_i[:]))
                step(v.memset(t["ones"][:], 1.0))
                step(v.memset(t["cell"][:], 0.0))
                step(v.tensor_tensor(lbm[:], lbl[:, 0, :], lbl[:, 1, :], ALU.max))
                step(v.tensor_tensor(lbl[:, 0, :], lbl[:, 0, :], lbm[:], ALU.subtract))
                step(v.tensor_tensor(lbl[:, 1, :], lbl[:, 1, :], lbm[:], ALU.subtract))
                col = lambda c: t["cols"][:, c:c + 1]
                step(v.tensor_scalar(ang[:], ang[:], col(C_INVF), None, ALU.mult))
                step(v.tensor_scalar(turns[:], ang[:], 1.0 / (2 * np.pi), col(C_TURN), ALU.mult, ALU.add))
                step(v.tensor_scalar(turns[:], turns[:], ROUND, None, ALU.add))
                step(v.tensor_scalar(turns[:], turns[:], -ROUND, None, ALU.add))
                for part in (PI2_A, PI2_B, PI2_C):
                    step(v.scalar_tensor_tensor(ang[:], turns[:], -part, ang[:], ALU.mult, ALU.add))
                step(v.tensor_scalar(ang[:], ang[:], col(C_RAD), None, ALU.add))
                step(v.tensor_scalar(ang[:], ang[:], 3.1415925, -3.1415925, ALU.min, ALU.max))
                v.wait_ge(act_steps, 1)
                step(v.tensor_tensor(lbs[:], lbe[:, 0, :], lbe[:, 1, :], ALU.add))
                step(v.reciprocal(lbs[:], lbs[:]))
                step(v.tensor_tensor(t["lb"][:], lbe[:, 0, :], lbs[:], ALU.mult))
                step(v.tensor_scalar(t["oml"][:], t["lb"][:], -1.0, 1.0, ALU.mult, ALU.add))
                step(v.tensor_scalar(t["noml"][:], t["oml"][:], -1.0, None, ALU.mult))
                v.wait_ge(act_steps, 2)
                step(v.tensor_scalar(t["trig"][:], t["trig"][:], col(C_SIGN), None, ALU.mult))


def phase_a(nc, t, d):
    with ExitStack() as ctx:
        sb = lambda name, shape, dt=F32: ctx.enter_context(nc.sbuf_tensor(name, shape, dt))
        sem = lambda name: ctx.enter_context(nc.semaphore(name))
        psum = lambda name: ctx.enter_context(nc.psum_tensor(name, [P, 512], F32))
        wi = t["wi"]
        xt = sb("xt", [P, 2, DM])
        xT = sb("xT", [P, KT, SPAN])
        gate = sb("gate", [P, HG, SPAN])
        key = sb("key", [P, HG, SPAN])
        logf = sb("logf", [P, HG, SPAN])
        ep = sb("ep", [P, HG, SPAN])
        en = sb("en", [P, HG, SPAN])
        qry = sb("qry", [P, HG, SPAN])
        gin = sb("gin", [P, HG, SPAN])
        sig = sb("sig", [P, HG, SPAN])
        ot = sb("ot", [P, HG, SPAN])
        rs = sb("rs", [P, HG, SPAN])
        vt = sb("vt", [P, 2, D_HG])
        kt = sb("kt", [P, 2, HG, P])
        am = sb("am", [P, 2, HG, P])
        state = sb("state", [P, 2, HG, P])
        lmx = sb("lmx", [P, HG, NC + 1])
        gsum = sb("gsum", [P, HG, NC])
        gf = sb("gf", [P, HG, NC])
        cqr = sb("cqr", [P, 3, SPAN])
        csq = sb("csq", [P, 3, SPAN])
        crs = sb("crs", [P, 2, SPAN])

        B = [psum(f"pa{i}") for i in range(4)]
        OB = [psum("po0"), psum("po1")]
        UB = [psum("pu0"), psum("pu1")]

        x_loaded = sem("x_loaded"); x_turned = sem("x_turned")
        xT_act = sem("xT_act"); xT_dve = sem("xT_dve"); projected = sem("projected")
        f_exp = sem("f_exp"); v_ready = sem("v_ready"); q_ready = sem("q_ready")
        g_raw = sem("g_raw"); g_exp = sem("g_exp"); c_raw = sem("c_raw"); c_sq = sem("c_sq"); kr_ready = sem("kr_ready")
        sig_f = sem("sig_f"); key_ready = sem("key_ready"); logf_ready = sem("logf_ready")
        cum = sem("cum"); carry = sem("carry"); gsum_ready = sem("gsum_ready"); gf_ready = sem("gf_ready"); centred = sem("centred")
        ep_ready = sem("ep_ready"); en_ready = sem("en_ready"); scaled = sem("scaled"); init = sem("a_init")
        k_turned = sem("k_turned"); kt_ready = sem("kt_ready"); a_done = sem("a_done"); a_ready = sem("a_ready")
        u_done = sem("u_done"); state_ready = sem("state_ready"); inter_done = sem("inter_done")
        o_ready = sem("o_ready"); osq = sem("osq"); o_sum = sem("o_sum"); o_root = sem("o_root"); c_sum = sem("c_sum"); c_root = sem("c_root")
        silu = sem("silu"); r_steps = sem("r_steps"); c_steps = sem("c_steps"); stored = sem("r_stored")

        xd = d["x"][0].rearrange("(s i p) n -> s p i n", p=P, i=2)
        rT = d["rT"].rearrange("(h p) n -> p h n", p=P)

        with nc.Block() as block:
            @block.sync
            def _(sp):
                sp.dma_start(xt[:], xd[0]).then_inc(x_loaded, 16)

                def span(m, last):
                    if not last:
                        sp.wait_ge(x_turned, m * 4 + 4)
                        sp.dma_start(xt[:], xd[m + 1]).then_inc(x_loaded, 16)
                    sp.wait_ge(r_steps, m * 3 + 3)
                    sp.dma_start(rT[:, :, bass.ds(m * SPAN, SPAN)], ot[:]).then_inc(stored, 16)
                with sp.Fori(0, NS - 1) as m:
                    span(m, False)
                span(NS - 1, True)
                sp.wait_ge(stored, 16 * NS)

            @block.tensor
            def _(pe):
                def turn_x(m):
                    pe.wait_ge(x_loaded, m * 16 + 16)
                    for n, b in enumerate((2, 3, 0, 1)):
                        for kk in range(2):
                            k = 2 * n + kk
                            for i in range(2):
                                ins = pe.transpose(B[b][:, kk * SPAN + i * P:kk * SPAN + (i + 1) * P],
                                                   xt[:, i, k * P:(k + 1) * P], t["ident"][:])
                        ins.then_inc(x_turned, 1)
                        yield n

                def project(b, col, m_cols):
                    for k in range(KT):
                        ins = pe.matmul(B[b][0:m_cols, 0:SPAN], wi[:, k, col:col + m_cols], xT[:, k, :],
                                        start=(k == 0), stop=(k == KT - 1))
                    ins.then_inc(projected, 1)

                for _ in turn_x(0):
                    pass
                pe.wait_ge(t["w_in_loaded"], 16 * KT)

                def span(m, last):
                    pe.wait_ge(xT_act, m * 2 + 2)
                    pe.wait_ge(xT_dve, m * 2 + 2)
                    pe.wait_ge(o_root, m * 2)
                    pe.wait_ge(a_ready, m * 2)
                    for h in range(HG):
                        project(h, W_F + h * P, P)
                    for i in range(2):
                        pe.wait_ge(f_exp, m * 4 + 1 + i)
                        for k in range(KT):
                            ins = pe.matmul(B[i][:], xT[:, k, i * P:(i + 1) * P], wi[:, k, W_I:W_I + D_HG],
                                            start=(k == 0), stop=(k == KT - 1))
                        ins.then_inc(projected, 1)
                    for h in range(HG):
                        if h < 2:
                            pe.wait_ge(f_exp, m * 4 + 3 + h)
                        else:
                            pe.wait_ge(v_ready, m * 2 + h - 1)
                        project((2 + h) % 4, W_Q + h * P, P)
                    for h in range(HG):
                        pe.wait_ge(q_ready, m * 4 + 1 + h)
                        project((2 + h) % 4, W_G + h * P, P)
                    pe.wait_ge(g_exp, m * 4 + 1)
                    project(2, W_CKV, P)
                    pe.wait_ge(g_exp, m * 4 + 2)
                    project(3, W_KR, 64)
                    pe.wait_ge(g_exp, m * 4 + 3)
                    project(0, W_CQ, P)
                    pe.wait_ge(g_exp, m * 4 + 4)
                    project(1, W_CQ + P, P)
                    if not last:
                        turning = turn_x(m + 1)
                        pe.wait_ge(c_raw, m * 3 + 1)
                        pe.wait_ge(c_sq, m * 3 + 1)
                        next(turning)
                        pe.wait_ge(kr_ready, m + 1)
                        next(turning)
                        pe.wait_ge(c_raw, m * 3 + 2)
                        pe.wait_ge(c_sq, m * 3 + 2)
                        next(turning)
                        pe.wait_ge(c_raw, m * 3 + 3)
                        pe.wait_ge(c_sq, m * 3 + 3)
                        next(turning)
                    else:
                        pe.wait_ge(c_sq, m * 3 + 3)
                        pe.wait_ge(c_raw, m * 3 + 3)
                        pe.wait_ge(kr_ready, m + 1)
                    pe.wait_ge(state_ready, m * NC)
                    for n, (lo, hi) in enumerate(((1, 3), (0, 1))):
                        for j in range(lo, hi):
                            ins = pe.matmul(UB[0][:, n * SPAN:(n + 1) * SPAN], t["ones"][:], csq[:, j, :],
                                            start=(j == lo), stop=(j == hi - 1))
                    ins.then_inc(c_sum, 1)
                    pe.wait_ge(scaled, m * 3 + 3)
                    if not last:
                        pe.wait_ge(xT_act, m * 2 + 4)
                        pe.wait_ge(xT_dve, m * 2 + 4)
                    for i in range(2):
                        for h in range(HG):
                            ins = pe.transpose(B[i][:, h * P:(h + 1) * P], key[:, h, i * P:(i + 1) * P], t["ident"][:])
                        ins.then_inc(k_turned, 1)
                        for h in range(HG):
                            ins = pe.matmul(B[2 + i][:, h * P:(h + 1) * P], key[:, h, i * P:(i + 1) * P],
                                            ep[:, h, i * P:(i + 1) * P], start=True, stop=True)
                        ins.then_inc(a_done, 1)
                    pe.wait_ge(kt_ready, m * 2 + 2)
                    pe.wait_ge(c_root, m * 2 + 2)

                    def update(c):
                        i, j = divmod(c, P // C)
                        if c >= 2:
                            pe.wait_ge(state_ready, m * NC + c - 1)
                        for h in range(HG):
                            ins = pe.matmul(UB[c % 2][:, h * P:(h + 1) * P], kt[j * C:(j + 1) * C, i, h, :],
                                            vt[j * C:(j + 1) * C, i, h * P:(h + 1) * P], start=True, stop=True,
                                            tile_position=(j * C, 0))
                        ins.then_inc(u_done, 1)

                    def inter(c):
                        i, j = divmod(c, P // C)
                        pe.wait_ge(state_ready, m * NC + c)
                        for h in range(HG):
                            ins = pe.matmul(OB[i][:, h * P + j * C:h * P + (j + 1) * C], state[:, (c + 1) % 2, h, :],
                                            qry[:, h, i * P + j * C:i * P + (j + 1) * C],
                                            start=False, stop=True, skip_group_check=True)
                        ins.then_inc(inter_done, 1)

                    update(0)
                    update(1)
                    for c in range(NC):
                        i, j = divmod(c, P // C)
                        if j == 0:
                            pe.wait_ge(a_ready, m * 2 + 1 + i)
                            pe.wait_ge(osq, m * 2 + i)
                            for h in range(HG):
                                pe.matmul(OB[i][:, h * P:(h + 1) * P], vt[:, i, h * P:(h + 1) * P], am[:, i, h, :],
                                          start=(h == 0), stop=False, skip_group_check=True)
                        inter(c)
                        if c + 2 < NC:
                            update(c + 2)
                    pe.wait_ge(osq, m * 2 + 2)
                    for n in range(2):
                        pe.matmul(B[n][:], t["ones"][:], en[:, 2 * n:2 * n + 2, :], start=True, stop=True).then_inc(o_sum, 1)
                with pe.Fori(0, NS - 1) as m:
                    span(m, False)
                span(NS - 1, True)

            @block.scalar
            def _(act):
                def xT_part(m):
                    for n in range(0, 4, 2):
                        act.wait_ge(x_turned, m * 4 + 1 + n)
                        nc.scalar.copy(xT[:, 2 * n:2 * n + 2, :], B[(2 + n) % 4][:].rearrange("p (k n) -> p k n", k=2)).then_inc(xT_act, 1)
                xT_part(0)

                def span(m, last):
                    act.wait_ge(scaled, m * 3)
                    act.wait_ge(key_ready, m * 4)
                    act.wait_ge(logf_ready, m * 4)
                    for h in range(HG):
                        act.wait_ge(projected, m * 18 + 1 + h)
                        nc.scalar.activation(gate[:, h, :], B[h][:, 0:SPAN], ACT.Exp, scale=-1.0).then_inc(f_exp, 1)
                    act.wait_ge(sig_f, m * 2 + 2)
                    act.wait_ge(r_steps, m * 3)
                    for h in range(HG):
                        nc.scalar.activation(logf[:, h, :], gate[:, h, :], ACT.Ln, bias=t["lb"][:, h:h + 1],
                                             scale=t["oml"][:, h:h + 1]).then_inc(logf_ready, 1)
                    act.wait_ge(k_turned, m * 2)
                    act.wait_ge(a_done, m * 2)
                    for h in range(HG):
                        nc.scalar.activation(key[:, h, :], gate[:, h, :], ACT.Identity, bias=t["oml"][:, h:h + 1],
                                             scale=t["noml"][:, h:h + 1]).then_inc(key_ready, 1)
                    act.wait_ge(gsum_ready, m + 1)
                    nc.scalar.activation(gf[:], gsum[:], ACT.Exp).then_inc(gf_ready, 1)
                    act.wait_ge(centred, m + 1)
                    act.wait_ge(a_done, m * 2)
                    nc.scalar.activation(ep[:], logf[:], ACT.Exp).then_inc(ep_ready, 1)
                    act.wait_ge(o_sum, m * 2)
                    nc.scalar.activation(en[:], logf[:], ACT.Exp, scale=-1.0).then_inc(en_ready, 1)
                    for h in range(HG):
                        act.wait_ge(projected, m * 18 + 11 + h)
                        b = B[(2 + h) % 4][:, 0:SPAN]
                        nc.scalar.copy(gin[:, h, :], b).then_inc(g_raw, 1)
                        nc.scalar.activation(sig[:, h, :], b, ACT.Exp, scale=-1.0).then_inc(g_exp, 1)
                    act.wait_ge(c_sum, m)
                    act.wait_ge(c_steps, m * 4)
                    for n, (p, b) in enumerate(((15, 2), (17, 0), (18, 1))):
                        act.wait_ge(projected, m * 18 + p)
                        nc.scalar.copy(cqr[:, n, :], B[b][:, 0:SPAN]).then_inc(c_raw, 1)
                        nc.scalar.square(csq[:, n, :], B[b][:, 0:SPAN]).then_inc(c_sq, 1)
                    if not last:
                        act.wait_ge(projected, m * 18 + 18)
                        xT_part(m + 1)
                    for i in range(2):
                        act.wait_ge(k_turned, m * 2 + 1 + i)
                        nc.scalar.copy(kt[:, i], B[i][:].rearrange("p (h n) -> p h n", h=HG)).then_inc(kt_ready, 1)
                    act.wait_ge(c_sum, m + 1)
                    act.wait_ge(c_steps, m * 4)
                    for n, rank in enumerate((Q_RANK, KV_RANK)):
                        nc.scalar.activation(crs[:, n, :], UB[0][:, n * SPAN:(n + 1) * SPAN], ACT.Sqrt, scale=1.0 / rank,
                                             bias=t["cols"][:, C_REPS:C_REPS + 1]).then_inc(c_root, 1)
                    act.wait_ge(stored, m * 16)
                    act.wait_ge(scaled, m * 3 + 3)
                    for i in range(2):
                        act.wait_ge(inter_done, m * NC + (i + 1) * NC // 2)
                        o = OB[i][:].rearrange("p (h n) -> p h n", h=HG)
                        nc.scalar.copy(ot[:, :, i * P:(i + 1) * P], o).then_inc(o_ready, 1)
                        nc.scalar.square(en[:, :, i * P:(i + 1) * P], o).then_inc(osq, 1)
                    for n in range(2):
                        act.wait_ge(o_sum, m * 2 + 1 + n)
                        nc.scalar.activation(rs[:, 2 * n:2 * n + 2, :], B[n][:].rearrange("p (h n) -> p h n", h=2), ACT.Sqrt,
                                             scale=1.0 / DK, bias=t["cols"][:, C_REPS:C_REPS + 1]).then_inc(o_root, 1)
                with act.Fori(0, NS - 1) as m:
                    span(m, False)
                span(NS - 1, True)

            @block.gpsimd
            def _(pool):
                nc.gpsimd.memset(state[:, 1], 0.0).then_inc(init, 1)
                nc.gpsimd.memset(lmx[:, :, NC:NC + 1], 0.0).then_inc(init, 1)

            @block.vector
            def _(v):
                def xT_part(m):
                    for n in range(1, 4, 2):
                        v.wait_ge(x_turned, m * 4 + 1 + n)
                        v.tensor_copy(xT[:, 2 * n:2 * n + 2, :], B[(2 + n) % 4][:].rearrange("p (k n) -> p k n", k=2)).then_inc(xT_dve, 1)
                xT_part(0)
                v.wait_ge(init, 2)

                def span(m, last):
                    v.wait_ge(f_exp, m * 4 + 4)
                    v.tensor_scalar(gate[:], gate[:], 1.0, None, ALU.add).then_inc(sig_f, 1)
                    v.wait_ge(sig_f, m * 2 + 1)
                    v.reciprocal(gate[:], gate[:]).then_inc(sig_f, 1)
                    v.wait_ge(logf_ready, m * 4 + 4)
                    flat = logf[:].rearrange("p h n -> p (h n)")
                    v.tensor_tensor_scan(flat, t["restart"][:], flat, 0.0, ALU.mult, ALU.add).then_inc(cum, 1)
                    v.tensor_copy(lmx[:, :, 0:1], lmx[:, :, NC:NC + 1]).then_inc(carry, 1)
                    v.wait_ge(cum, m + 1)
                    v.wait_ge(carry, m * 2 + 1)
                    b4 = logf[:].rearrange("p h (c s) -> p h c s", s=C)
                    v.tensor_tensor(lmx[:, :, 1:NC + 1], b4[:, :, :, C - 1], b4[:, :, :, C // 2 - 1], ALU.subtract).then_inc(carry, 1)
                    v.wait_ge(carry, m * 2 + 2)
                    v.wait_ge(gf_ready, m)
                    v.tensor_tensor(gsum[:], b4[:, :, :, C // 2 - 1], lmx[:, :, 0:NC], ALU.add).then_inc(gsum_ready, 1)
                    v.wait_ge(gsum_ready, m + 1)
                    v.tensor_copy(gsum2[:], b4[:, :, :, C // 2 - 1]).then_inc(mid_ready, 1)
                    v.wait_ge(mid_ready, m + 1)
                    bc = logf[:].rearrange("p h (c s) -> p (h c) s", s=C)
                    mid = gsum2[:].rearrange("p h c -> p (h c)").unsqueeze(2).broadcast_to([P, HG * NC, C])
                    v.tensor_tensor(bc, bc, mid, ALU.subtract).then_inc(centred, 1)
                    for i in range(2):
                        v.wait_ge(projected, m * 18 + 5 + i)
                        if i == 0:
                            v.wait_ge(inter_done, m * NC)
                        v.tensor_copy(vt[:, i, :], B[i][:]).then_inc(v_ready, 1)
                    for h in range(HG):
                        v.wait_ge(projected, m * 18 + 7 + h)
                        v.tensor_copy(qry[:, h, :], B[(2 + h) % 4][:, 0:SPAN]).then_inc(q_ready, 1)
                    v.wait_ge(q_ready, m * 4 + 4)
                    v.wait_ge(ep_ready, m + 1)
                    v.tensor_tensor(ep[:], qry[:], ep[:], ALU.mult).then_inc(scaled, 1)
                    v.wait_ge(key_ready, m * 4 + 4)
                    v.wait_ge(en_ready, m + 1)
                    v.tensor_tensor(key[:], key[:], en[:], ALU.mult).then_inc(scaled, 1)
                    v.wait_ge(gf_ready, m + 1)
                    v.wait_ge(scaled, m * 3 + 1)
                    v.tensor_tensor(qry[:].rearrange("p h (c s) -> p (h c) s", s=C), ep[:].rearrange("p h (c s) -> p (h c) s", s=C),
                                    gf[:].rearrange("p h c -> p (h c)").unsqueeze(2).broadcast_to([P, HG * NC, C]),
                                    ALU.mult).then_inc(scaled, 1)
                    v.wait_ge(g_exp, m * 4 + 4)
                    v.tensor_scalar(sig[:], sig[:], 1.0, None, ALU.add).then_inc(silu, 1)
                    v.wait_ge(silu, m * 3 + 1)
                    v.reciprocal(sig[:], sig[:]).then_inc(silu, 1)
                    v.wait_ge(silu, m * 3 + 2)
                    v.wait_ge(g_raw, m * 4 + 4)
                    v.tensor_tensor(gin[:], gin[:], sig[:], ALU.mult).then_inc(silu, 1)
                    v.wait_ge(projected, m * 18 + 16)
                    v.tensor_tensor(t["krp"][0:64, bass.ds(m * SPAN, SPAN)], B[3][0:64, 0:SPAN],
                                    t["trig"][0:64, bass.ds(m * SPAN, SPAN)], ALU.mult).then_inc(kr_ready, 1)
                    if not last:
                        v.wait_ge(projected, m * 18 + 18)
                        xT_part(m + 1)
                    for i in range(2):
                        v.wait_ge(a_done, m * 2 + 1 + i)
                        v.scalar_tensor_tensor(am[:, i], B[2 + i][:].rearrange("p (h n) -> p h n", h=HG), 3.0e38,
                                               t["causal"][:].unsqueeze(1).broadcast_to([P, HG, P]),
                                               ALU.min, ALU.mult).then_inc(a_ready, 1)
                    for c in range(NC):
                        v.wait_ge(u_done, m * NC + 1 + c)
                        v.wait_ge(inter_done, m * NC + c)
                        v.wait_ge(state_ready, m * NC + c)
                        for h in range(HG):
                            ins = v.scalar_tensor_tensor(state[:, c % 2, h, :], state[:, (c + 1) % 2, h, :], gf[:, h, c:c + 1],
                                                         UB[c % 2][:, h * P:(h + 1) * P], ALU.mult, ALU.add)
                        ins.then_inc(state_ready, 1)
                    v.wait_ge(c_root, m * 2 + 2)
                    v.reciprocal(crs[:], crs[:]).then_inc(c_steps, 1)
                    v.wait_ge(c_steps, m * 4 + 1)
                    v.wait_ge(c_raw, m * 3 + 3)
                    for j in range(2):
                        v.scalar_tensor_tensor(t["cqn"][:, j, bass.ds(m * SPAN, SPAN)], cqr[:, 1 + j, :], t["gq"][:, j:j + 1],
                                               crs[:, 0, :], ALU.mult, ALU.mult).then_inc(c_steps, 1)
                    v.scalar_tensor_tensor(t["ckvn"][:, bass.ds(m * SPAN, SPAN)], cqr[:, 0, :], t["gkv"][:, 0:1],
                                           crs[:, 1, :], ALU.mult, ALU.mult).then_inc(c_steps, 1)
                    v.wait_ge(o_root, m * 2 + 2)
                    v.reciprocal(rs[:], rs[:]).then_inc(r_steps, 1)
                    v.wait_ge(r_steps, m * 3 + 1)
                    v.wait_ge(o_ready, m * 2 + 2)
                    v.scalar_tensor_tensor(ot[:], ot[:], t["ghg"][:, 0:1], rs[:], ALU.mult, ALU.mult).then_inc(r_steps, 1)
                    v.wait_ge(r_steps, m * 3 + 2)
                    v.wait_ge(silu, m * 3 + 3)
                    v.tensor_tensor(ot[:], ot[:], gin[:], ALU.mult).then_inc(r_steps, 1)
                gsum2 = sb("gsum2", [P, HG, NC])
                mid_ready = sem("mid_ready")
                with v.Fori(0, NS - 1) as m:
                    span(m, False)
                span(NS - 1, True)


QT_ORDER = [q for i in range(NT // 2) for q in (i, NT - 1 - i)]
ITEMS = [(x, q) for x in range(2) for q in QT_ORDER]
BANKS = [(q + 4) // 4 for _, q in ITEMS]
FIRST_BANK = [sum(BANKS[:n]) for n in range(len(ITEMS) + 1)]
NI, NBK = len(ITEMS), FIRST_BANK[len(ITEMS)]


def phase_b(nc, t, d):
    with ExitStack() as ctx:
        sb = lambda name, shape, dt=F32: ctx.enter_context(nc.sbuf_tensor(name, shape, dt))
        sem = lambda name: ctx.enter_context(nc.semaphore(name))
        psum = lambda name, n=512: ctx.enter_context(nc.psum_tensor(name, [P, n], F32))
        wq = sb("wq", [P, 2, 2, P])
        wk = sb("wk", [P, 2, NOPE])
        wv = sb("wv", [P, 2, VD])
        qT = sb("qT", [P, 2, SEQ])
        kT = sb("kT", [P, 2, SEQ])
        vp = sb("vp", [P, NT, 2 * VD])
        pr = sb("pr", [P, 2, SEQ])
        prT = sb("prT", [P, 2, NT, P])
        mx = sb("mx", [P, NI, 4])
        mxa = sb("mxa", [P, NI])
        nmx = sb("nmx", [P, NI])
        rsum = sb("rsum", [P, NI, 4])
        rsa = sb("rsa", [P, NI])
        rin = sb("rin", [P, NI])
        S = [psum(f"pS{i}") for i in range(4)]
        TB = [psum(f"pT{i}") for i in range(2)]
        OB = [psum(f"pO{i}") for i in range(2)]
        w_loaded = sem("w_loaded"); folded = sem("folded"); rope_copied = sem("rope_copied")
        prep = sem("prep"); prep_act = sem("prep_act"); prep_dve = sem("prep_dve")
        s_done = sem("s_done"); masked = sem("masked"); mx_part = sem("mx_part"); mx_all = sem("mx_all"); nmx_ready = sem("nmx_ready")
        exp_done = sem("exp_done"); t_done = sem("t_done"); t_dve = sem("t_dve"); t_act = sem("t_act")
        pv_done = sem("pv_done"); rs_ready = sem("rs_ready"); rin_ready = sem("rin_ready"); o_out = sem("o_out")
        wq_d = d["w_uq"].rearrange("g (k p) x c -> g p k x c", p=P)
        wkv_d = d["w_ukv"]
        PREP = [("k", x, c) for x in range(2) for c in range(4)] + [("q", x, c) for x in range(2) for c in range(4)] + \
               [("v", 0, c) for c in range(4)]
        NP = len(PREP)

        with nc.Block() as block:
            @block.sync
            def _(sp):
                with sp.Fori(0, HEADS // 2) as g:
                    sp.wait_ge(prep, g * NP)
                    sp.dma_start(wq[:], wq_d[g]).then_inc(w_loaded, 16)
                    sp.dma_start(wk[:], wkv_d[g, 0]).then_inc(w_loaded, 16)
                    sp.dma_start(wv[:], wkv_d[g, 1]).then_inc(w_loaded, 16)

            @block.tensor
            def _(pe):
                for c in range(4):
                    ins = pe.matmul(S[c][64:128, :], t["fold"][0:64, 64:128], t["krp"][0:64, c * 512:(c + 1) * 512],
                                    start=True, stop=True, tile_position=(0, 64))
                    ins.then_inc(folded, 1)

                with pe.Fori(0, HEADS // 2) as g:
                    pe.wait_ge(w_loaded, g * 48 + 48)
                    pe.wait_ge(exp_done, g * NBK)
                    pe.wait_ge(rope_copied, 8)
                    for n, (kind, x, c) in enumerate(PREP):
                        if n >= 4:
                            pe.wait_ge(prep_act, g * NP + n - 3)
                        if n >= 8:
                            pe.wait_ge(prep_dve, g * 8 + min(n - 4 - 8 + 1, 8)) if n >= 12 else None
                        b = S[n % 4]
                        if kind == "k":
                            ins = pe.matmul(b[0:64, :], wk[:, x, :], t["ckvn"][:, c * 512:(c + 1) * 512], start=True, stop=True)
                        elif kind == "q":
                            for k in range(2):
                                ins = pe.matmul(b[:], wq[:, k, x, :], t["cqn"][:, k, c * 512:(c + 1) * 512],
                                                start=(k == 0), stop=(k == 1))
                        else:
                            for i in range(4):
                                ins = pe.matmul(b[:, i * P:(i + 1) * P], t["ckvn"][:, (4 * c + i) * P:(4 * c + i + 1) * P],
                                                wv[:].rearrange("p x c -> p (x c)"), start=True, stop=True)
                        ins.then_inc(prep, 1)
                    pe.wait_ge(prep_act, g * NP + NP)
                    pe.wait_ge(prep_dve, g * 8 + 8)

                    def turn(n, gr):
                        x, q = ITEMS[n]
                        u = FIRST_BANK[n] + gr
                        if gr == 0:
                            pe.wait_ge(exp_done, g * NBK + FIRST_BANK[n + 1])
                        if u >= 2:
                            pe.wait_ge(t_dve if u % 2 == 0 else t_act, g * (NBK // 2) + u // 2)
                        for i in range(min(4, q + 1 - 4 * gr)):
                            kt_ = 4 * gr + i
                            ins = pe.transpose(TB[u % 2][:, i * P:(i + 1) * P], pr[:, n % 2, kt_ * P:(kt_ + 1) * P], t["ident"][:])
                        ins.then_inc(t_done, 1)

                    def weigh(n, gr):
                        x, q = ITEMS[n]
                        u = FIRST_BANK[n] + gr
                        if gr == 0 and n >= 2:
                            pe.wait_ge(o_out, g * NI + n - 1)
                        pe.wait_ge(t_dve if u % 2 == 0 else t_act, g * (NBK // 2) + u // 2 + 1)
                        for i in range(min(4, q + 1 - 4 * gr)):
                            kt_ = 4 * gr + i
                            ins = pe.matmul(OB[n % 2][:, 0:VD], prT[:, n % 2, kt_, :], vp[:, kt_, x * VD:(x + 1) * VD],
                                            start=(kt_ == 0), stop=(kt_ == q))
                        if gr == BANKS[n] - 1:
                            ins.then_inc(pv_done, 1)

                    pe.wait_ge(o_out, g * NI)
                    pe.wait_ge(t_dve, g * (NBK // 2))
                    pe.wait_ge(t_act, g * (NBK // 2))
                    for n in range(NI + 2):
                        if n < NI:
                            x, q = ITEMS[n]
                            for j in range(BANKS[n]):
                                u = FIRST_BANK[n] + j
                                if u >= 4:
                                    pe.wait_ge(exp_done, g * NBK + u - 3)
                                w = min(512, (q + 1) * P - j * 512)
                                pe.matmul(S[u % 4][:, 0:w], qT[:, x, q * P:(q + 1) * P], kT[:, x, j * 512:j * 512 + w],
                                          start=True, stop=True).then_inc(s_done, 1)
                        turns = BANKS[n - 1] if 1 <= n <= NI else 0
                        weighs = BANKS[n - 2] if n >= 2 else 0
                        for gr in range(4):
                            if gr < turns:
                                turn(n - 1, gr)
                            if gr < weighs:
                                weigh(n - 2, gr)

            @block.scalar
            def _(act):
                for c in range(4):
                    act.wait_ge(folded, c + 1)
                    for x in range(2):
                        nc.scalar.copy(kT[64:128, x, c * 512:(c + 1) * 512], S[c][64:128, :]).then_inc(rope_copied, 1)

                with act.Fori(0, HEADS // 2) as g:
                    act.wait_ge(pv_done, g * NI)
                    for n, (kind, x, c) in enumerate(PREP):
                        act.wait_ge(prep, g * NP + n + 1)
                        b = S[n % 4]
                        if kind == "k":
                            ins = nc.scalar.copy(kT[0:64, x, c * 512:(c + 1) * 512], b[0:64, :])
                        elif kind == "q":
                            ins = nc.scalar.copy(qT[0:64, x, c * 512:(c + 1) * 512], b[0:64, :])
                        else:
                            ins = nc.scalar.copy(vp[:, 4 * c:4 * c + 4, :], b[:].rearrange("p (i c) -> p i c", i=4))
                        ins.then_inc(prep_act, 1)
                    for n in range(NI + 1):
                        if n < NI:
                            x, q = ITEMS[n]
                            if n >= 2:
                                act.wait_ge(t_done, g * NBK + FIRST_BANK[n - 1])
                            act.wait_ge(nmx_ready, g * NI + n + 1)
                            for j in range(BANKS[n]):
                                u = FIRST_BANK[n] + j
                                w = min(512, (q + 1) * P - j * 512)
                                nc.scalar.activation(pr[:, n % 2, j * 512:j * 512 + w], S[u % 4][:, 0:w], ACT.Exp, scale=SCALE,
                                                     bias=nmx[:, n:n + 1], accum_out=rsum[:, n, j:j + 1]).then_inc(exp_done, 1)
                        if n >= 1:
                            m = n - 1
                            for gr in range(BANKS[m]):
                                u = FIRST_BANK[m] + gr
                                if u % 2 == 1:
                                    w = min(4, ITEMS[m][1] + 1 - 4 * gr)
                                    act.wait_ge(t_done, g * NBK + u + 1)
                                    if m >= 2:
                                        act.wait_ge(pv_done, g * NI + m - 1)
                                    nc.scalar.copy(prT[:, m % 2, 4 * gr:4 * gr + w, :],
                                                   TB[1][:, 0:w * P].rearrange("p (i c) -> p i c", i=w)).then_inc(t_act, 1)

            @block.vector
            def _(v):
                with v.Fori(0, HEADS // 2) as g:
                    v.wait_ge(pv_done, g * NI)
                    for n, (kind, x, c) in enumerate(PREP):
                        if kind == "q":
                            v.wait_ge(prep, g * NP + n + 1)
                            v.tensor_tensor(qT[64:128, x, c * 512:(c + 1) * 512], S[n % 4][64:128, :],
                                            t["trig"][64:128, c * 512:(c + 1) * 512], ALU.mult).then_inc(prep_dve, 1)
                    for n in range(NI + 2):
                        if n < NI:
                            x, q = ITEMS[n]
                            nb = BANKS[n]
                            v.wait_ge(exp_done, g * NBK)
                            for j in range(nb):
                                u = FIRST_BANK[n] + j
                                w = min(512, (q + 1) * P - j * 512)
                                v.wait_ge(s_done, g * NBK + u + 1)
                                if j == nb - 1:
                                    v.memset(S[u % 4][0:64, w - 64:w], -3.0e38).then_inc(masked, 1)
                                    v.wait_ge(masked, g * NI + n + 1)
                                v.tensor_reduce(mx[:, n, j:j + 1], S[u % 4][:, 0:w], AX, ALU.max).then_inc(mx_part, 1)
                            v.wait_ge(mx_part, g * NBK + FIRST_BANK[n + 1])
                            v.tensor_reduce(mxa[:, n:n + 1], mx[:, n, 0:nb], AX, ALU.max).then_inc(mx_all, 1)
                            v.wait_ge(mx_all, g * NI + n + 1)
                            v.tensor_scalar(nmx[:, n:n + 1], mxa[:, n:n + 1], -SCALE, None, ALU.mult).then_inc(nmx_ready, 1)
                        if 1 <= n <= NI:
                            m = n - 1
                            for gr in range(BANKS[m]):
                                u = FIRST_BANK[m] + gr
                                if u % 2 == 0:
                                    w = min(4, ITEMS[m][1] + 1 - 4 * gr)
                                    v.wait_ge(t_done, g * NBK + u + 1)
                                    if m >= 2:
                                        v.wait_ge(pv_done, g * NI + m - 1)
                                    v.tensor_copy(prT[:, m % 2, 4 * gr:4 * gr + w, :],
                                                  TB[0][:, 0:w * P].rearrange("p (i c) -> p i c", i=w)).then_inc(t_dve, 1)
                        if n >= 2:
                            m = n - 2
                            x, q = ITEMS[m]
                            v.wait_ge(exp_done, g * NBK + FIRST_BANK[m + 1])
                            v.tensor_reduce(rsa[:, m:m + 1], rsum[:, m, 0:BANKS[m]], AX, ALU.add).then_inc(rs_ready, 1)
                            v.wait_ge(rs_ready, g * NI + m + 1)
                            v.reciprocal(rin[:, m:m + 1], rsa[:, m:m + 1]).then_inc(rin_ready, 1)
                            v.wait_ge(pv_done, g * NI + m + 1)
                            v.wait_ge(rin_ready, g * NI + m + 1)
                            v.tensor_scalar(t["ao"][:, q, bass.ds(g * (2 * VD) + x * VD, VD)], OB[m % 2][:, 0:VD],
                                            rin[:, m:m + 1], None, ALU.mult).then_inc(o_out, 1)


def phase_c(nc, t, d):
    with ExitStack() as ctx:
        sb = lambda name, shape, dt=F32: ctx.enter_context(nc.sbuf_tensor(name, shape, dt))
        sem = lambda name: ctx.enter_context(nc.semaphore(name))
        psum = lambda name, n=512: ctx.enter_context(nc.psum_tensor(name, [P, n], F32))
        wo = sb("wo", [P, KT, DM])
        wr = sb("wr", [P, KT, NG + NE])
        rb = sb("rb", [P, NG + NE])
        ga = sb("ga", [P, 4])
        g1 = sb("g1", [P, DM])
        b1 = sb("b1", [P, DM])
        rts = sb("rts", [P, 4, 2 * P])
        xs = sb("xs", [P, 2, DM])
        ap = sb("ap", [P, 2, 512])
        asq = sb("asq", [P, 2, 512])
        ass = sb("ass", [P, 2])
        ars = sb("ars", [P, 2])
        an = sb("an", [P, 2, 512])
        anT = sb("anT", [P, 2, 4, P])
        hp = sb("hp", [P, 2, DM])
        st = sb("st", [P, 2, 2, 6])
        mv = sb("mv", [P, 2, 2])
        sd = sb("sd", [P, 2])
        rstd = sb("rstd", [P, 2])
        hT = sb("hT", [P, 2, KT, P])
        A = [psum(f"cA{i}") for i in range(1)]
        M = [psum(f"cM{i}") for i in range(4)]
        H = [psum(f"cH{i}") for i in range(2)]
        L = psum("cL")
        c_loaded = sem("c_loaded"); scaled = sem("wo_scaled"); r_loaded = sem("r_loaded"); x_loaded = sem("xc_loaded")
        a_picked = sem("a_picked"); a_sum = sem("a_sum"); a_root = sem("a_root"); a_rs = sem("a_rs"); a_norm = sem("a_norm"); a_turned = sem("a_turned"); anT_ready = sem("anT_ready")
        mixed = sem("mixed"); res = sem("res"); stats = sem("stats"); aggr = sem("aggr"); root = sem("root"); rstd_ready = sem("rstd_ready")
        normed = sem("normed"); h_steps = sem("h_steps"); h_ready = sem("h_ready"); stored = sem("h_stored")
        h_turned = sem("h_turned"); hT_dve = sem("hT_dve"); hT_act = sem("hT_act"); l_done = sem("l_done"); l_ready = sem("l_ready")
        rT = d["rT"].rearrange("(h p) n -> p h n", p=P)
        xd = d["x"][0].rearrange("(s i p) n -> s p i n", p=P, i=2)
        hd = d["h"].rearrange("(s i p) n -> s i p n", p=P, i=2)
        STEPS = NT // 2
        with nc.Block() as block:
            @block.sync
            def _(sp):
                w = d["w_out"][0].rearrange("(k p) n -> p k n", p=P)
                for dst, src in ((ga[:], d["mla_out_g"]), (wo[:, 0:4], w[:, 0:4]), (wo[:, 4:8], w[:, 4:8]),
                                 (wr[:], d["w_router"].rearrange("(k p) n -> p k n", p=P)),
                                 (rb[:], d["b_router"].broadcast_to([P, NG + NE])),
                                 (g1[:], d["ln1_g"].broadcast_to([P, DM])), (b1[:], d["ln1_b"].broadcast_to([P, DM]))):
                    sp.dma_start(dst, src).then_inc(c_loaded, 16)
                sp.dma_start(rts[:], rT[:, :, 0:2 * P]).then_inc(r_loaded, 16)
                sp.dma_start(xs[:], xd[0]).then_inc(x_loaded, 16)

                def step(m, last):
                    for i in range(2):
                        if i == 1 and not last:
                            sp.wait_ge(mixed, m * 2 + 2)
                            sp.dma_start(rts[:], rT[:, :, bass.ds((m + 1) * 2 * P, 2 * P)]).then_inc(r_loaded, 16)
                            sp.wait_ge(res, m * 4 + 4)
                            sp.dma_start(xs[:], xd[m + 1]).then_inc(x_loaded, 16)
                        sp.wait_ge(h_ready, m * 2 + 1 + i)
                        sp.dma_start(hd[m, i], hp[:, i]).then_inc(stored, 16)
                with sp.Fori(0, STEPS - 1) as m:
                    step(m, False)
                step(STEPS - 1, True)
                sp.wait_ge(stored, 16 * NT)

            @block.tensor
            def _(pe):
                def project(m, i):
                    pe.wait_ge(anT_ready, m * 2 + i + 1)
                    pe.wait_ge(res, m * 4 + 2 * i)
                    for part in range(2):
                        if part == 1:
                            pe.wait_ge(r_loaded, m * 16 + 16)
                        for half in range(2):
                            for k in range(4):
                                lhs = anT[:, i, k, :] if part == 0 else rts[:, k, i * P:(i + 1) * P]
                                ins = pe.matmul(M[2 * i + half][:], lhs, wo[:, 4 * part + k, half * 512:(half + 1) * 512],
                                                start=(part == 0 and k == 0), stop=(part == 1 and k == 3))
                    ins.then_inc(mixed, 1)

                def route(n, i):
                    pe.wait_ge(h_ready, n + 1)
                    pe.wait_ge(hT_dve, n)
                    pe.wait_ge(hT_act, n)
                    for half in range(2):
                        for k in range(4):
                            ins = pe.transpose(H[half][:, k * P:(k + 1) * P], hp[:, i, (4 * half + k) * P:(4 * half + k + 1) * P], t["ident"][:])
                        ins.then_inc(h_turned, 1)

                def logits(n, i):
                    pe.wait_ge(hT_dve, n + 1)
                    pe.wait_ge(hT_act, n + 1)
                    pe.wait_ge(l_ready, n)
                    for k in range(KT):
                        ins = pe.matmul(L[:, 0:NG + NE], hT[:, i, k, :], wr[:, k, :], start=(k == 0), stop=(k == KT - 1))
                    ins.then_inc(l_done, 1)

                def step(m, first):
                    for i in range(2):
                        pe.wait_ge(a_norm, m * 2 + i + 1)
                        pe.wait_ge(anT_ready, m * 2 + i)
                        for k in range(4):
                            ins = pe.transpose(A[0][:, k * P:(k + 1) * P], an[:, i, k * P:(k + 1) * P], t["ident"][:])
                        ins.then_inc(a_turned, 1)
                        if i == 0 and not first:
                            route(m * 2 - 1, 1)
                    project(m, 0)
                    if not first:
                        logits(m * 2 - 1, 1)
                    project(m, 1)
                    route(m * 2, 0)
                    logits(m * 2, 0)
                pe.wait_ge(c_loaded, 7 * 16)
                pe.wait_ge(scaled, 4)
                step(0, True)
                with pe.Fori(1, STEPS) as m:
                    step(m, False)
                route(NT - 1, 1)
                logits(NT - 1, 1)

            @block.scalar
            def _(act):
                act.wait_ge(c_loaded, 7 * 16)
                for k in range(4):
                    nc.scalar.activation(wo[:, k], wo[:, k], ACT.Identity, scale=ga[:, k:k + 1]).then_inc(scaled, 1)

                def turned(n, i):
                    act.wait_ge(h_turned, 2 * n + 2)
                    act.wait_ge(l_done, n)
                    nc.scalar.copy(hT[:, i, 4:8, :], H[1][:].rearrange("p (k n) -> p k n", k=4)).then_inc(hT_act, 1)

                def step(m, first):
                    for i in range(2):
                        act.wait_ge(a_sum, m * 2 + i)
                        act.wait_ge(a_picked, m * 2 + 1 + i)
                        nc.scalar.activation(asq[:, i, :], ap[:, i, :], ACT.Square,
                                             accum_out=ass[:, i:i + 1]).then_inc(a_sum, 1)
                    act.wait_ge(a_sum, m * 2 + 2)
                    act.wait_ge(a_rs, m)
                    nc.scalar.activation(ars[:], ass[:], ACT.Sqrt, scale=1.0 / 512, bias=t["cols"][:, C_REPS:C_REPS + 1]).then_inc(a_root, 1)
                    for i in range(2):
                        act.wait_ge(a_rs, m + 1)
                        act.wait_ge(a_turned, m * 2)
                        nc.scalar.activation(an[:, i, :], ap[:, i, :], ACT.Copy, scale=ars[:, i:i + 1]).then_inc(a_norm, 1)
                    for i in range(2):
                        act.wait_ge(a_turned, m * 2 + 1 + i)
                        act.wait_ge(mixed, m * 2)
                        nc.scalar.copy(anT[:, i], A[0][:].rearrange("p (k n) -> p k n", k=4)).then_inc(anT_ready, 1)
                        if i == 0 and not first:
                            turned(m * 2 - 1, 1)
                    for i in range(2):
                        act.wait_ge(aggr, m * 2 + 1 + i)
                        act.wait_ge(rstd_ready, m * 2)
                        nc.scalar.activation(sd[:, i:i + 1], mv[:, i, 1:2], ACT.Sqrt, bias=t["cols"][:, C_LEPS:C_LEPS + 1]).then_inc(root, 1)
                    turned(m * 2, 0)
                step(0, True)
                with act.Fori(1, STEPS) as m:
                    step(m, False)
                turned(NT - 1, 1)

            @block.gpsimd
            def _(pool):
                with pool.Fori(0, STEPS) as m:
                    for i in range(2):
                        pool.wait_ge(h_steps, m * 4 + 2 * i + 2)
                        nc.gpsimd.tensor_tensor(hp[:, i], hp[:, i], b1[:], ALU.add).then_inc(h_ready, 1)

            @block.vector
            def _(v):
                hold = Hold("memset", t["cell"], sem("hold_c"))

                def turned(n, i):
                    v.wait_ge(h_turned, 2 * n + 1)
                    v.wait_ge(l_done, n)
                    v.tensor_copy(hT[:, i, 0:4, :], H[0][:].rearrange("p (k n) -> p k n", k=4)).then_inc(hT_dve, 1)

                def logged(n):
                    v.wait_ge(l_done, n + 1)
                    v.tensor_tensor(t["lg"][:, bass.ds(n, 1), :], L[:, 0:NG + NE].unsqueeze(1), rb[:].unsqueeze(1), ALU.add).then_inc(l_ready, 1)

                v.wait_ge(c_loaded, 7 * 16)

                def pick(m):
                    v.wait_ge(a_norm, m * 2)
                    v.tensor_scalar(ap[:], t["ao"][:, bass.ds(m * 2, 2), :], 1.0, None, ALU.mult).then_inc(a_picked, 2)

                def step(m, first):
                    pick(m)
                    v.wait_ge(a_root, m + 1)
                    v.reciprocal(ars[:], ars[:]).then_inc(a_rs, 1)
                    if not first:
                        turned(m * 2 - 1, 1)
                        logged(m * 2 - 1)
                    for i in range(2):
                        v.wait_ge(mixed, m * 2 + 1 + i)
                        v.wait_ge(x_loaded, m * 16 + 16)
                        v.wait_ge(stored, (m * 2 + i) * 16)
                        v.wait_ge(h_turned, m * 4 + 0)
                        for half in range(2):
                            sl = slice(half * 512, (half + 1) * 512)
                            v.scalar_tensor_tensor(hp[:, i, sl], xs[:, i, sl], ALPHA, M[2 * i + half][:], ALU.mult, ALU.add).then_inc(res, 1)
                        for half in range(2):
                            v.wait_ge(res, m * 4 + 2 * i + half + 1)
                            v.bn_stats(st[:, i, half, :], hp[:, i, half * 512:(half + 1) * 512]).then_inc(stats, 1)
                        v.wait_ge(stats, m * 4 + 2 * i + 2)
                        hold(v, m * 2 + i)
                        v.bn_aggr(mv[:, i, :], st[:, i]).then_inc(aggr, 1)
                        v.wait_ge(root, m * 2 + i + 1)
                        v.reciprocal(rstd[:, i:i + 1], sd[:, i:i + 1]).then_inc(rstd_ready, 1)
                        v.wait_ge(rstd_ready, m * 2 + i + 1)
                        v.tensor_scalar(hp[:, i], hp[:, i], mv[:, i, 0:1], rstd[:, i:i + 1], ALU.subtract, ALU.mult).then_inc(h_steps, 1)
                        v.wait_ge(h_steps, m * 4 + 2 * i + 1)
                        v.tensor_tensor(hp[:, i], hp[:, i], g1[:], ALU.mult).then_inc(h_steps, 1)
                    turned(m * 2, 0)
                    logged(m * 2)
                step(0, True)
                with v.Fori(1, STEPS) as m:
                    step(m, False)
                turned(NT - 1, 1)
                logged(NT - 1)


def phase_d(nc, t, d):
    with ExitStack() as ctx:
        sb = lambda name, shape, dt=F32: ctx.enter_context(nc.sbuf_tensor(name, shape, dt))
        sem = lambda name: ctx.enter_context(nc.semaphore(name))
        rows = sb("d_rows", [P, 2 * NE + NBP])
        before = sb("d_before", [P, P])
        restart = sb("d_restart", [P, NE * NT])
        token = sb("d_token", [P, NT], I32)
        gmax = sb("gmax", [P, NT]); gexp = sb("gexp", [P, NT, NG]); geq = sb("geq", [P, NT, NG])
        gidx = sb("gidx", [P, NT]); pgrp = sb("pgrp", [P, NT])
        e1 = sb("e1", [P, NT, NE]); e2 = sb("e2", [P, NT, NE]); eq = sb("eq", [P, NT, NE])
        m1 = sb("m1", [P, NT]); m2 = sb("m2", [P, NT]); ix = sb("ix", [P, NT]); ee = sb("ee", [P, NT]); de = sb("de", [P, NT])
        oh = sb("oh", [P, 2, NT, NE]); both = sb("both", [P, NT, NE])
        tot = sb("tot", [P, NE, NT]); inc = sb("inc", [P, NE, NT]); rank = sb("rank", [P, NT, NE])
        nblk = sb("nblk", [P, NE]); bend = sb("bend", [P, NE]); bbeg = sb("bbeg", [P, NE])
        blk = sb("blk", [P, NBP, NE]); bex = sb("bex", [P, NBP]); new = sb("new", [P, NBP])
        slot = sb("slot", [P, NT, 2]); bq = sb("bq", [P, NT, 2]); pos = sb("pos", [P, NT, 2]); posi = sb("posi", [P, NT, 2], U32)
        zero = sb("zero", [P, NBP], I32)
        wt = ctx.enter_context(nc.psum_tensor("dW", [P, 512], F32))
        al = ctx.enter_context(nc.psum_tensor("dA", [P, 512], F32))
        loaded = sem("d_loaded"); steps = sem("dve_d_steps"); exps = sem("d_exps"); ranks = sem("d_ranks")
        cleared = sem("cleared"); scattered = sem("scattered"); read = sem("slots_read"); at = {}
        with nc.Block() as block:
            @block.vector
            def _(v):
                n = [0]

                def step(ins, name=None):
                    n[0] += 1
                    ins.then_inc(steps, 1)
                    if name:
                        at[name] = n[0]
                    v.wait_ge(steps, n[0])
                bc = lambda a, k: a.unsqueeze(2).broadcast_to([P, NT, k])
                row = lambda a, b: rows[:, a:b].unsqueeze(1).broadcast_to([P, NT, b - a])
                G, E = t["lg"][:, :, 0:NG], t["lg"][:, :, NG:NG + NE]
                step(v.memset(zero[:], 0), "zero")
                v.wait_ge(loaded, 64)
                step(v.tensor_reduce(gmax[:], G, AX, ALU.max))
                step(v.tensor_tensor(gexp[:], G, bc(gmax[:], NG), ALU.subtract), "gexp")
                step(v.tensor_tensor(geq[:], G, bc(gmax[:], NG), ALU.is_equal))
                step(v.tensor_scalar(geq[:], geq[:], -64.0, 64.0, ALU.mult, ALU.add))
                step(v.tensor_tensor(geq[:], geq[:], row(R_EXPERT, R_EXPERT + NG), ALU.add))
                step(v.tensor_reduce(gidx[:], geq[:], AX, ALU.min))
                step(v.tensor_tensor(eq[:], row(R_GROUP, R_GROUP + NE), bc(gidx[:], NE), ALU.is_equal))
                step(v.tensor_tensor(e1[:], E, eq[:], ALU.mult))
                step(v.tensor_scalar(eq[:], eq[:], BIG, -BIG, ALU.mult, ALU.add))
                step(v.tensor_tensor(e1[:], e1[:], eq[:], ALU.add))
                for k, (src, m) in enumerate(((e1, m1), (e2, m2))):
                    step(v.tensor_reduce(m[:], src[:], AX, ALU.max))
                    step(v.tensor_tensor(eq[:], src[:], bc(m[:], NE), ALU.is_equal))
                    step(v.tensor_scalar(eq[:], eq[:], -64.0, 64.0, ALU.mult, ALU.add))
                    step(v.tensor_tensor(eq[:], eq[:], row(R_EXPERT, R_EXPERT + NE), ALU.add))
                    step(v.tensor_reduce(ix[:], eq[:], AX, ALU.min))
                    step(v.tensor_tensor(oh[:, k], row(R_EXPERT, R_EXPERT + NE), bc(ix[:], NE), ALU.is_equal))
                    if k == 0:
                        step(v.scalar_tensor_tensor(e2[:], oh[:, 0], -BIG, e1[:], ALU.mult, ALU.add))
                step(v.tensor_tensor(both[:], oh[:, 0], oh[:, 1], ALU.add), "both")
                step(v.tensor_tensor(de[:], m2[:], m1[:], ALU.subtract), "de")
                v.wait_ge(exps, 2)
                step(v.tensor_reduce(pgrp[:], gexp[:], AX, ALU.add))
                step(v.tensor_scalar(de[:], ee[:], 1.0, None, ALU.add))
                step(v.tensor_tensor(pgrp[:], pgrp[:], de[:], ALU.mult))
                step(v.reciprocal(pgrp[:], pgrp[:]))
                step(v.tensor_copy(t["gates"][:, :, 0], pgrp[:]))
                step(v.tensor_tensor(t["gates"][:, :, 1], pgrp[:], ee[:], ALU.mult))
                v.wait_ge(ranks, 2)
                step(v.tensor_copy(tot[:], al[:].rearrange("p (n e) -> p e n", e=NE)))
                flat = lambda a: a[:].rearrange("p a b -> p (a b)")
                step(v.tensor_tensor_scan(flat(inc), restart[:], flat(tot), 0.0, ALU.mult, ALU.add))
                step(v.tensor_tensor(tot[:], inc[:], tot[:], ALU.subtract))
                step(v.tensor_scalar(nblk[:], inc[:, :, NT - 1], 1.0 / P, (P - 1.0) / P - 0.49609375, ALU.mult, ALU.add))
                step(v.tensor_scalar(nblk[:], nblk[:], ROUND, None, ALU.add))
                step(v.tensor_scalar(nblk[:], nblk[:], -ROUND, None, ALU.add))
                step(v.tensor_tensor_scan(bend[:], t["ones"][:, 0:NE], nblk[:], 0.0, ALU.mult, ALU.add))
                step(v.tensor_tensor(bbeg[:], bend[:], nblk[:], ALU.subtract))
                step(v.tensor_scalar(bbeg[:], bbeg[:], float(P), None, ALU.mult))
                step(v.tensor_tensor(rank[:], wt[:].rearrange("p (n e) -> p n e", e=NE), tot[:].rearrange("p e n -> p n e"), ALU.add))
                step(v.tensor_tensor(rank[:], rank[:], bbeg[:].unsqueeze(1).broadcast_to([P, NT, NE]), ALU.add))
                for k in range(2):
                    step(v.tensor_tensor(eq[:], oh[:, k], rank[:], ALU.mult))
                    step(v.tensor_reduce(slot[:, :, k], eq[:], AX, ALU.add))
                step(v.tensor_copy(t["slots"][:], slot[:]))
                step(v.tensor_scalar(bq[:], slot[:], 1.0 / P, -0.49609375, ALU.mult, ALU.add))
                step(v.tensor_scalar(bq[:], bq[:], ROUND, None, ALU.add))
                step(v.tensor_scalar(bq[:], bq[:], -ROUND, None, ALU.add))
                step(v.tensor_scalar(pos[:], slot[:], float(NBP), None, ALU.mult))
                step(v.scalar_tensor_tensor(pos[:], bq[:], 1.0 - float(P * NBP), pos[:], ALU.mult, ALU.add))
                step(v.tensor_copy(posi[:], pos[:]), "posi")
                step(v.tensor_tensor(blk[:], bend[:].unsqueeze(1).broadcast_to([P, NBP, NE]),
                                     rows[:, R_BLOCK:R_BLOCK + NBP].unsqueeze(2).broadcast_to([P, NBP, NE]), ALU.is_le))
                step(v.tensor_reduce(bex[:], blk[:], AX, ALU.add))
                step(v.tensor_scalar(bex[:], bex[:], NE - 1.0, None, ALU.min))
                step(v.tensor_copy(t["bexp"][:], bex[:]))
                step(v.tensor_scalar(t["last"][:], bend[:, NE - 1:NE], -1.0, None, ALU.add))
                step(v.memset(new[:], 1.0))
                step(v.tensor_tensor(new[:, 1:], bex[:, 1:], bex[:, :NBP - 1], ALU.not_equal))
                step(v.tensor_tensor(bex[:], rows[:, R_BLOCK:R_BLOCK + NBP], bend[:, NE - 1:NE].broadcast_to([P, NBP]), ALU.is_lt))
                step(v.tensor_tensor(new[:], new[:], bex[:], ALU.mult))
                step(v.tensor_tensor_scan(bex[:], t["ones"][:, 0:NBP], new[:], 0.0, ALU.mult, ALU.add))
                step(v.tensor_copy(t["ord"][:], bex[:]))

            @block.scalar
            def _(act):
                act.wait_ge(steps, at["gexp"])
                nc.scalar.activation(gexp[:], gexp[:], ACT.Exp).then_inc(exps, 1)
                act.wait_ge(steps, at["de"])
                nc.scalar.activation(ee[:], de[:], ACT.Exp).then_inc(exps, 1)

            @block.tensor
            def _(pe):
                pe.wait_ge(steps, at["both"])
                b = both[:].rearrange("p n e -> p (n e)")
                pe.matmul(wt[:], before[:], b, start=True, stop=True).then_inc(ranks, 1)
                pe.matmul(al[:], t["ones"][:], b, start=True, stop=True).then_inc(ranks, 1)

            @block.sync
            def _(sp):
                for dst, src in ((rows, "rows"), (before, "before"), (restart, "restart_tiles"), (token, "token")):
                    sp.dma_start(dst[:], d[src]).then_inc(loaded, 16)
                sp.wait_ge(steps, at["zero"])
                sp.dma_start(d["slot_tok"].rearrange("(p b) o -> p (b o)", p=P), zero[:]).then_inc(cleared, 16)
                sp.wait_ge(scattered, 16 * 2 * NT)
                sp.dma_start(t["tok"][:], d["slot_tok"].rearrange("(p b) o -> p (b o)", p=P)).then_inc(read, 16)
                sp.wait_ge(read, 16)

            @block.gpsimd
            def _(pool):
                pool.wait_ge(cleared, 16)
                pool.wait_ge(steps, at["posi"])
                for n in range(NT):
                    for k in range(2):
                        nc.gpsimd.indirect_dma_start(
                            out=d["slot_tok"], out_offset=bass.IndirectOffsetOnAxis(ap=posi[:, n, k:k + 1], axis=0),
                            in_=token[:, n:n + 1], in_offset=None).then_inc(scattered, 16)


def phase_e(nc, t, d):
    with ExitStack() as ctx:
        sb = lambda name, shape, dt=F32: ctx.enter_context(nc.sbuf_tensor(name, shape, dt))
        sem = lambda name: ctx.enter_context(nc.semaphore(name))
        psum = lambda name, n=512: ctx.enter_context(nc.psum_tensor(name, [P, n], F32))

        class Weights:

            def __init__(self, name, k, n):
                self.src = d[name][0].rearrange("e (k p) n -> e p k n", p=P)
                self.raw = sb(name + "_raw", [P, k, n])
                self.hi, self.lo = sb(name + "_hi", [P, k, n], F32R), sb(name + "_lo", [P, k, n], F32R)
                self.loaded = sem(name + "_loaded")
                self.hi_ready, self.lo_ready = sem(name + "_hi_ready"), sem(name + "_lo_ready")
                self.used = sem(name + "_used")
        w1, w3, w2 = Weights("w1", KT, DE), Weights("w3", KT, DE), Weights("w2", DE // P, DM)
        idx = sb("idx", [P, 1], U32)
        xg = sb("xg", [P, DM])
        xh = sb("xh", [P, KT, P], F32R); xl = sb("xl", [P, KT, P], F32R)
        up = sb("up", [P, DE])
        uh = sb("uh", [P, DE // P, P], F32R); ul = sb("ul", [P, DE // P, P], F32R)
        y = sb("y", [P, DM])
        blank = sb("blank", [P, DM])
        X = [psum("eX0"), psum("eX1")]; U = psum("eU"); H1 = psum("eH1"); H3 = psum("eH3"); Y = [psum("eY0"), psum("eY1")]
        idx_ready = sem("idx_ready"); gathered = sem("gathered"); x_turned = sem("xg_turned"); xh_ready = sem("xh_ready"); xl_ready = sem("xl_ready")
        silu = sem("silu_done"); gated = sem("gated"); up_turned = sem("up_turned"); uh_ready = sem("uh_ready"); ul_ready = sem("ul_ready")
        y_dve = sem("y_dve"); y_act = sem("y_act"); stored = sem("y_stored"); held = sem("hold_e"); blanked = sem("blanked")
        yd = d["y"].rearrange("(b p) n -> b p n", p=P)
        four = lambda a: a.rearrange("p (k n) -> p k n", k=4)

        def cell(eng, name, b):
            top = {"ord": NE, "bexp": NE - 1, "last": NB - 1}[name]
            col = t[name][0:1, b:b + 1] if isinstance(b, int) else t[name][0:1, bass.ds(b, 1)]
            return eng.value_load(col, min_val={"ord": 1, "bexp": 0, "last": SEQ * 2 // P - 1}[name], max_val=top)

        def blocks(eng, stage):
            last = cell(eng, "last", 0)
            stage(0)
            stage(1)
            with eng.Fori(2, NB) as b:
                with eng.If(b <= last):
                    stage(b)
            return last

        def where_new(eng, b, act):
            o, before = cell(eng, "ord", b), cell(eng, "ord", b - 1)
            with eng.If(o > before):
                act(o, before)

        with nc.Block() as block:
            @block.sync
            def _(sp):
                def load(w, b, before):
                    e = cell(sp, "bexp", b)
                    if before is not None:
                        sp.wait_ge(w.lo_ready, before)
                    sp.dma_start(w.raw[:], w.src[bass.ds(e, 1)].rearrange("o p k n -> p (o k) n")).then_inc(w.loaded, 16)
                def other(b, *ws):
                    where_new(sp, b, lambda o, before: [load(w, b, before) for w in ws])

                def stage(b):
                    if isinstance(b, int) and b == 0:
                        load(w1, 0, None)
                        load(w3, 0, None)
                        return
                    other(b, w1, w3)
                    if isinstance(b, int) and b == 1:
                        load(w2, 0, None)
                    else:
                        other(b - 1, w2)
                last = blocks(sp, stage)
                other(last, w2)

            @block.gpsimd
            def _(pool):
                hold = Hold("add", t["cell"], held)

                def gather(b):
                    if not isinstance(b, int) or b > 0:
                        pool.wait_ge(x_turned, b * 2)
                    pool.wait_ge(idx_ready, b + 1)
                    hold(nc.gpsimd, b)
                    nc.gpsimd.indirect_dma_start(out=xg[:], out_offset=None, in_=d["h"],
                                                 in_offset=bass.IndirectOffsetOnAxis(ap=idx[:], axis=0)).then_inc(gathered, 16)
                last = blocks(pool, gather)
                gather(last + 1)

            @block.tensor
            def _(pe):
                def turn_x(b):
                    pe.wait_ge(gathered, b * 16 + 16)
                    if not isinstance(b, int) or b > 0:
                        pe.wait_ge(xh_ready, b * 2)
                        pe.wait_ge(xl_ready, b * 2)
                    for k in range(KT):
                        ins = pe.transpose(X[k // 4][:, (k % 4) * P:(k % 4 + 1) * P], xg[:, k * P:(k + 1) * P], t["ident"][:])
                        if k % 4 == 3:
                            ins.then_inc(x_turned, 1)

                def first(b):
                    o = cell(pe, "ord", b)
                    for w, H, free in ((w1, H1, silu), (w3, H3, gated)):
                        if not isinstance(b, int) or b > 0:
                            pe.wait_ge(free, b)
                        pe.wait_ge(w.hi_ready, o)
                        if w is w1:
                            pe.wait_ge(xh_ready, b * 2 + 2)
                            pe.wait_ge(xl_ready, b * 2 + 2)
                        for k in range(KT):
                            pe.matmul(H[:], xh[:, k, :], w.hi[:, k, :], start=(k == 0), stop=False)
                            pe.matmul(H[:], xl[:, k, :], w.hi[:, k, :], start=False, stop=False)
                        pe.wait_ge(w.lo_ready, o)
                        for k in range(KT):
                            ins = pe.matmul(H[:], xh[:, k, :], w.lo[:, k, :], start=False, stop=(k == KT - 1))
                        ins.then_inc(w.used, 1)

                def second(b):
                    o = cell(pe, "ord", b)
                    if not isinstance(b, int) or b > 0:
                        pe.wait_ge(y_dve, b)
                        pe.wait_ge(y_act, b)
                    pe.wait_ge(uh_ready, b + 1)
                    pe.wait_ge(ul_ready, b + 1)
                    pe.wait_ge(w2.hi_ready, o)
                    K2 = DE // P
                    for half in range(2):
                        at = slice(half * 512, (half + 1) * 512)
                        for k in range(K2):
                            pe.matmul(Y[half][:], uh[:, k, :], w2.hi[:, k, at], start=(k == 0), stop=False)
                            pe.matmul(Y[half][:], ul[:, k, :], w2.hi[:, k, at], start=False, stop=False)
                    pe.wait_ge(w2.lo_ready, o)
                    for half in range(2):
                        at = slice(half * 512, (half + 1) * 512)
                        for k in range(K2):
                            ins = pe.matmul(Y[half][:], uh[:, k, :], w2.lo[:, k, at], start=False, stop=(k == K2 - 1))
                    ins.then_inc(w2.used, 1)

                def turn_up(b):
                    pe.wait_ge(gated, b + 1)
                    for k in range(DE // P):
                        ins = pe.transpose(U[:, k * P:(k + 1) * P], up[:, k * P:(k + 1) * P], t["ident"][:])
                    ins.then_inc(up_turned, 1)

                def stage(b):
                    first(b)
                    turn_x(b + 1)
                    if not isinstance(b, int) or b > 0:
                        second(b - 1)
                    turn_up(b)
                turn_x(0)
                second(blocks(pe, stage))

            def split_hi(act, w, b):
                def split(o, before=0):
                    act.wait_ge(w.loaded, o * 16)
                    if not isinstance(b, int) or b > 0:
                        act.wait_ge(w.used, b)
                    nc.scalar.copy(w.hi[:], w.raw[:]).then_inc(w.hi_ready, 1)
                if isinstance(b, int) and b == 0:
                    split(1)
                else:
                    where_new(act, b, split)

            def split_lo(v, w, b):
                def split(o, before=0):
                    v.wait_ge(w.hi_ready, o)
                    if not isinstance(b, int) or b > 0:
                        v.wait_ge(w.used, b)
                    v.tensor_tensor(w.lo[:], w.raw[:], w.hi[:].bitcast(F32), ALU.subtract).then_inc(w.lo_ready, 1)
                if isinstance(b, int) and b == 0:
                    split(1)
                else:
                    where_new(v, b, split)

            @block.scalar
            def _(act):
                def x_part(b):
                    for n in range(2):
                        act.wait_ge(x_turned, b * 2 + 1 + n)
                        if not isinstance(b, int) or b > 0:
                            act.wait_ge(w3.used, b)
                        nc.scalar.copy(xh[:, 4 * n:4 * n + 4, :], four(X[n][:])).then_inc(xh_ready, 1)

                def y_part(b):
                    act.wait_ge(w2.used, b + 1)
                    if not isinstance(b, int) or b > 0:
                        act.wait_ge(stored, b * 16)
                    nc.scalar.copy(y[:, 512:], Y[1][:]).then_inc(y_act, 1)
                    act.wait_ge(y_dve, b + 1)
                    act.wait_ge(y_act, b + 1)
                    act.dma_start(yd[b], y[:]).then_inc(stored, 16)

                def stage(b):
                    later = not isinstance(b, int) or b > 0
                    if later:
                        split_hi(act, w2, b - 1)
                    act.wait_ge(w1.used, b + 1)
                    if later:
                        act.wait_ge(up_turned, b)
                    nc.scalar.activation(up[:], H1[:], ACT.Silu).then_inc(silu, 1)
                    split_hi(act, w1, b + 1)
                    x_part(b + 1)
                    split_hi(act, w3, b + 1)
                    if later:
                        y_part(b - 1)
                    act.wait_ge(up_turned, b + 1)
                    if later:
                        act.wait_ge(w2.used, b)
                    nc.scalar.copy(uh[:], four(U[:])).then_inc(uh_ready, 1)
                split_hi(act, w1, 0)
                x_part(0)
                split_hi(act, w3, 0)
                last = blocks(act, stage)
                split_hi(act, w2, last)
                y_part(last)
                act.wait_ge(blanked, 1)
                with act.Fori(2, NB) as b:
                    with act.If(b > last):
                        act.dma_start(yd[b], blank[:]).then_inc(stored, 16)
                act.wait_ge(stored, NB * 16)

            @block.vector
            def _(v):
                def index(b):
                    if not isinstance(b, int) or b > 0:
                        v.wait_ge(gathered, b * 16)
                        v.tensor_scalar(idx[:], t["tok"][:, bass.ds(b, 1)], 0.0, None, ALU.add).then_inc(idx_ready, 1)
                    else:
                        v.tensor_scalar(idx[:], t["tok"][:, 0:1], 0.0, None, ALU.add).then_inc(idx_ready, 1)

                def x_part(b):
                    for n in range(2):
                        v.wait_ge(xh_ready, b * 2 + 1 + n)
                        v.tensor_tensor(xl[:, 4 * n:4 * n + 4, :], four(X[n][:]), xh[:, 4 * n:4 * n + 4, :].bitcast(F32),
                                        ALU.subtract).then_inc(xl_ready, 1)

                def y_part(b):
                    v.wait_ge(w2.used, b + 1)
                    if not isinstance(b, int) or b > 0:
                        v.wait_ge(stored, b * 16)
                    v.tensor_copy(y[:, 0:512], Y[0][:]).then_inc(y_dve, 1)

                def stage(b):
                    later = not isinstance(b, int) or b > 0
                    index(b + 1)
                    if later:
                        split_lo(v, w2, b - 1)
                    split_lo(v, w1, b + 1)
                    v.wait_ge(silu, b + 1)
                    v.wait_ge(w3.used, b + 1)
                    v.tensor_tensor(up[:], up[:], H3[:], ALU.mult).then_inc(gated, 1)
                    x_part(b + 1)
                    split_lo(v, w3, b + 1)
                    if later:
                        y_part(b - 1)
                    v.wait_ge(uh_ready, b + 1)
                    v.tensor_tensor(ul[:], four(U[:]), uh[:].bitcast(F32), ALU.subtract).then_inc(ul_ready, 1)
                v.memset(blank[:], 0.0).then_inc(blanked, 1)
                index(0)
                split_lo(v, w1, 0)
                x_part(0)
                split_lo(v, w3, 0)
                last = blocks(v, stage)
                split_lo(v, w2, last)
                y_part(last)


def phase_f(nc, t, d):
    TS = 4
    with ExitStack() as ctx:
        sb = lambda name, shape, dt=F32: ctx.enter_context(nc.sbuf_tensor(name, shape, dt))
        sem = lambda name: ctx.enter_context(nc.semaphore(name))
        g2 = sb("g2", [P, DM]); b2 = sb("b2", [P, DM])
        idx = sb("fidx", [P, TS, 2], U32); gt = sb("fgt", [P, TS, 2])
        yg = sb("yg", [P, TS, 2, DM]); hs = sb("fhs", [P, TS, DM])
        st = sb("fst", [P, TS, 2, 6]); mv = sb("fmv", [P, TS, 2]); sd = sb("fsd", [P, TS]); rstd = sb("frstd", [P, TS]); nmr = sb("fnmr", [P, TS])
        loaded = sem("f_loaded"); idx_ready = sem("f_idx"); gt_ready = sem("f_gt"); got = [sem(f"f_got{i}") for i in range(TS)]
        h_loaded = [sem(f"f_h{i}") for i in range(TS)]; first = sem("f_first"); second = sem("f_second"); stats = sem("f_stats"); aggr = sem("f_aggr")
        root = sem("f_root"); rst = sem("f_rst"); nm = sem("f_nm"); normed = sem("f_normed"); scaled = sem("f_scaled"); done = sem("f_done"); stored = [sem(f"f_stored{i}") for i in range(TS)]
        held = sem("hold_f"); held_v = sem("hold_fv")
        hd = d["h"].rearrange("(m i p) n -> m i p n", i=TS, p=P)
        od = d["out"][0].rearrange("(m i p) n -> m i p n", i=TS, p=P)
        M = NT // TS
        with nc.Block() as block:
            @block.sync
            def _(sp):
                sp.dma_start(g2[:], d["ln2_g"].broadcast_to([P, DM])).then_inc(loaded, 16)
                sp.dma_start(b2[:], d["ln2_b"].broadcast_to([P, DM])).then_inc(loaded, 16)
                for i in range(TS):
                    sp.dma_start(hs[:, i], hd[0, i]).then_inc(h_loaded[i], 16)

                def step(m, last):
                    for i in range(TS):
                        sp.wait_ge(done, m * TS + i + 1)
                        sp.dma_start(od[m, i], yg[:, i, 0]).then_inc(stored[i], 16)
                        if not last:
                            sp.wait_ge(second, (m * TS + i) * 2 + 2)
                            sp.dma_start(hs[:, i], hd[m + 1, i]).then_inc(h_loaded[i], 16)
                with sp.Fori(0, M - 1) as m:
                    step(m, False)
                step(M - 1, True)
                for i in range(TS):
                    sp.wait_ge(stored[i], 16 * M)

            @block.gpsimd
            def _(pool):
                hold = Hold("add", t["cell"], held)
                pool.wait_ge(loaded, 32)

                def gather(m, i):
                    pool.wait_ge(idx_ready, m + 1)
                    pool.wait_ge(stored[i], m * 16)
                    hold(nc.gpsimd, m * TS + i)
                    for k in range(2):
                        nc.gpsimd.indirect_dma_start(out=yg[:, i, k], out_offset=None, in_=d["y"],
                                                     in_offset=bass.IndirectOffsetOnAxis(ap=idx[:, i, k:k + 1], axis=0)).then_inc(got[i], 16)

                def shift(m, i):
                    pool.wait_ge(scaled, m * TS + i + 1)
                    nc.gpsimd.tensor_tensor(yg[:, i, 0], yg[:, i, 0], b2[:], ALU.add).then_inc(done, 1)
                for i in range(TS):
                    gather(0, i)

                with pool.Fori(0, M - 1) as m:
                    for i in range(TS):
                        shift(m, i)
                        if i >= 1:
                            gather(m + 1, i - 1)
                    gather(m + 1, TS - 1)
                for i in range(TS):
                    shift(M - 1, i)

            @block.scalar
            def _(act):
                with act.Fori(0, M) as m:
                    act.wait_ge(gt_ready, m + 1)
                    for i in range(TS + 1):
                        if i < TS:
                            act.wait_ge(got[i], m * 32 + 32)
                            nc.scalar.activation(yg[:, i, 0], yg[:, i, 0], ACT.Copy, scale=gt[:, i, 0:1]).then_inc(first, 1)
                        if i >= 1:
                            j = i - 1
                            act.wait_ge(aggr, m * TS + j + 1)
                            act.wait_ge(rst, m * TS)
                            nc.scalar.activation(sd[:, j:j + 1], mv[:, j, 1:2], ACT.Sqrt, bias=t["cols"][:, C_LEPS:C_LEPS + 1]).then_inc(root, 1)
                            act.wait_ge(nm, m * TS + j + 1)
                            nc.scalar.activation(yg[:, j, 0], yg[:, j, 1], ACT.Identity, scale=rstd[:, j:j + 1],
                                                 bias=nmr[:, j:j + 1]).then_inc(normed, 1)

            @block.vector
            def _(v):
                hold = Hold("memset", t["cell"], held_v)
                v.wait_ge(loaded, 32)

                def pick(m):
                    if not isinstance(m, int):
                        for i in range(TS):
                            v.wait_ge(got[i], m * 32)
                    v.tensor_scalar(idx[:], t["slots"][:, bass.ds(m * TS, TS), :], 0.0, None, ALU.add).then_inc(idx_ready, 1)
                pick(0)

                def step(m, last):
                    v.wait_ge(normed, m * TS)
                    v.tensor_scalar(gt[:], t["gates"][:, bass.ds(m * TS, TS), :], 1.0, None, ALU.mult).then_inc(gt_ready, 1)
                    v.wait_ge(gt_ready, m + 1)
                    for i in range(TS + 1):
                        if i < TS:
                            n = m * TS + i
                            v.wait_ge(first, n + 1)
                            v.scalar_tensor_tensor(yg[:, i, 1], yg[:, i, 1], gt[:, i, 1:2], yg[:, i, 0], ALU.mult, ALU.add).then_inc(second, 1)
                            v.wait_ge(second, n * 2 + 1)
                            v.wait_ge(h_loaded[i], m * 16 + 16)
                            v.scalar_tensor_tensor(yg[:, i, 1], hs[:, i], ALPHA, yg[:, i, 1], ALU.mult, ALU.add).then_inc(second, 1)
                            v.wait_ge(second, n * 2 + 2)
                            for half in range(2):
                                v.bn_stats(st[:, i, half], yg[:, i, 1, half * 512:(half + 1) * 512]).then_inc(stats, 1)
                            v.wait_ge(stats, n * 2 + 2)
                            hold(v, n)
                            v.bn_aggr(mv[:, i], st[:, i]).then_inc(aggr, 1)
                        if i >= 1:
                            j = i - 1
                            n = m * TS + j
                            v.wait_ge(root, n + 1)
                            v.reciprocal(rstd[:, j:j + 1], sd[:, j:j + 1]).then_inc(rst, 1)
                            v.wait_ge(rst, n + 1)
                            v.scalar_tensor_tensor(nmr[:, j:j + 1], mv[:, j, 0:1], -1.0, rstd[:, j:j + 1], ALU.mult, ALU.mult).then_inc(nm, 1)
                        if i == TS and not last:
                            pick(m + 1)
                        if i >= 1:
                            v.wait_ge(normed, n + 1)
                            v.tensor_tensor(yg[:, j, 0], yg[:, j, 0], g2[:], ALU.mult).then_inc(scaled, 1)
                with v.Fori(0, M - 1) as m:
                    step(m, False)
                step(M - 1, True)


def build(nc, d):
    with ExitStack() as ctx:
        t = {}

        def keep(ctx, name, shape, dt=F32):
            t[name] = ctx.enter_context(nc.sbuf_tensor(name, shape, dt))
        for name in ("ident", "fold", "causal", "ones"):
            keep(ctx, name, [P, P])
        keep(ctx, "cols", [P, 8])
        keep(ctx, "cell", [P, 8])
        keep(ctx, "lg", [P, NT, NG + NE])
        t["w_in_loaded"] = ctx.enter_context(nc.semaphore("w_in_loaded"))
        with ExitStack() as attn:
            keep(attn, "trig", [P, SEQ])
            keep(attn, "cqn", [P, 2, SEQ])
            keep(attn, "ckvn", [P, SEQ])
            keep(attn, "krp", [P, SEQ])
            for name, n in (("gq", 2), ("gkv", 1)):
                keep(attn, name, [P, n])
            with ExitStack() as proj:
                keep(proj, "wi", [P, KT, W_COLS])
                keep(proj, "restart", [P, HG * SPAN])
                for name, n in (("ghg", 1), ("lb", HG), ("oml", HG), ("noml", HG)):
                    keep(proj, name, [P, n])
                phase_0(nc, t, d)
                phase_a(nc, t, d)
            keep(attn, "ao", [P, NT, HEADS * VD])
            phase_b(nc, t, d)
            phase_c(nc, t, d)
        route_and_experts(nc, t, d)


def route_and_experts(nc, t, d):
    with ExitStack() as ctx:
        for name, shape, dt in (("gates", [P, NT, 2], F32), ("slots", [P, NT, 2], U32),
                                ("tok", [P, NBP], I32), ("bexp", [P, NBP], I32), ("ord", [P, NBP], I32), ("last", [P, 1], I32)):
            t[name] = ctx.enter_context(nc.sbuf_tensor(name, shape, dt))
        phase_d(nc, t, d)
        phase_e(nc, t, d)
        phase_f(nc, t, d)


INPUTS = ("x", "positions", "w_in", "q_norm_g", "w_uq", "kv_norm_g", "w_ukv", "mla_out_g", "hg_lb_logits", "hg_norm_g",
          "w_out", "ln1_g", "ln1_b", "w_router", "b_router", "w1", "w3", "w2", "ln2_g", "ln2_b")
SCRATCH = (("rT", (D_HG, SEQ), F32), ("h", (SEQ, DM), F32), ("y", (NB * P, DM), F32), ("slot_tok", (NBP * P, 1), I32))


def kernel(**inputs):
    import concourse.bacc as bacc
    from concourse.bass_utils import run_bass_kernel_spmd as run

    laid = lay_out(inputs)
    arrays = {n: laid[n] for n in INPUTS}
    arrays.update(shape_constants())
    arrays = {"in_" + n: np.ascontiguousarray(a) for n, a in arrays.items()}
    nc = bacc.Bacc("TRN2", target_bir_lowering=False, num_devices=1)
    d = {n[3:]: nc.dram_tensor(n, a.shape, mybir.dt.from_np(a.dtype), kind="ExternalInput").ap() for n, a in arrays.items()}
    for name, shape, dt in SCRATCH:
        d[name] = nc.dram_tensor("scratch_" + name, shape, dt, kind="Internal").ap()
    d["out"] = nc.dram_tensor("out", (1, SEQ, DM), F32, kind="ExternalOutput").ap()
    build(nc, d)
    r = run(nc, [arrays], core_ids=[0])
    return r.results[0]["out"]
```

```python
from contextlib import ExitStack

import numpy as np
import concourse.bass as bass
from concourse import mybir

F32 = mybir.dt.float32
I32 = mybir.dt.int32
U32 = mybir.dt.uint32
F32R = mybir.dt.float32r
ALU = mybir.AluOpType
ACT = mybir.ActivationFunctionType
AX = mybir.AxisListType.X

P = 128
SEQ, DM = 2048, 1024
KT = DM // P
Q_RANK, KV_RANK, ROPE = 256, 128, 32
NOPE, VD, HEADS = 64, 64, 8
HG, DK = 4, 128
D_HG = HG * DK
NG, EPG = 4, 8
NE = NG * EPG
DE = 512
NT = SEQ // P
ALPHA = 2.0 ** 0.25
RMS_EPS, LN_EPS = 1e-6, 1e-5
SCALE = (NOPE + ROPE) ** -0.5
NB = (SEQ * 2 + NE * (P - 1)) // P
FIELD = 64
LEAST = SEQ * 2 // P
NBP = NB + 2

SPAN = 256
NS = SEQ // SPAN
C = 32
NC = SPAN // C

W_CQ, W_CKV, W_KR, W_F = 0, 256, 384, 448
W_I, W_Q, W_G = W_F + 512, W_F + 1024, W_F + 1536
W_COLS = W_F + 2048
W_PARTS = ((W_F, W_I), (W_I, W_Q), (W_Q, W_G), (W_G, W_COLS), (0, W_F))

C_INVF, C_TURN, C_RAD, C_SIGN, C_REPS, C_LEPS = range(6)

R_EXPERT, R_GROUP, R_BLOCK = 0, NE, 2 * NE
BIG = 3.0e38

PI2_A = 6.28125
PI2_B = float(np.float32(round((2 * np.pi - PI2_A) * 2.0 ** 21) / 2.0 ** 21))
PI2_C = float(np.float32(2 * np.pi - PI2_A - PI2_B))
ROUND = 12582912.0


class Hold:

    def __init__(self, op, cell, sem):
        self.op, self.cell, self.sem = op, cell, sem

    def __call__(self, eng, before):
        eng.wait_ge(self.sem, before)
        if self.op == "memset":
            ins = eng.memset(self.cell[:, 0:1], 0.0)
        else:
            ins = eng.tensor_tensor(self.cell[:, 3:4], self.cell[:, 4:5], self.cell[:, 4:5], ALU.add)
        ins.then_inc(self.sem, 1)


def since(eng, sem, count):
    if not isinstance(count, int) or count > 0:
        eng.wait_ge(sem, count)


def shape_constants():
    c = {}
    c["ident"] = np.eye(P, dtype=np.float32)
    s = np.arange(P)
    c["causal"] = ((s[:, None] <= s[None, :]) & (s[:, None] // C == s[None, :] // C)).astype(np.float32)
    c["before"] = (s[:, None] < s[None, :]).astype(np.float32)
    col = np.zeros((P, 8), np.float32)
    freq = (np.float32(10000.0) ** (-(np.arange(0, ROPE, 2, dtype=np.float32) / np.float32(ROPE)))).astype(np.float32)
    j = s % 64
    col[:, C_INVF] = freq[j % 16]
    col[:, C_TURN] = np.where(j < 32, 0.25, 0.0)
    col[:, C_RAD] = np.where(j < 32, np.pi / 2, 0.0)
    col[:, C_SIGN] = np.where((j >= 32) & (j < 48), -1.0, 1.0)
    col[:, C_REPS] = RMS_EPS
    col[:, C_LEPS] = LN_EPS
    c["cols"] = col
    fold = np.zeros((P, P), np.float32)
    fold[:64, 64:] = (s[:64, None] % 32 == s[None, :64] % 32)
    c["fold"] = fold
    c["restart_tiles"] = np.tile((np.arange(NT * NE) % NT != 0).astype(np.float32), (P, 1))
    row = np.zeros((P, 2 * NE + P), np.float32)
    row[:, R_EXPERT:R_EXPERT + NE] = np.arange(NE)
    row[:, R_GROUP:R_GROUP + NE] = np.arange(NE) // EPG
    row[:, R_BLOCK:R_BLOCK + P] = np.arange(P)
    c["rows"] = row
    c["token"] = (np.arange(NT)[None, :] * P + s[:, None]).astype(np.float32)
    c["restart"] = np.tile((np.arange(HG * SPAN) % C != 0).astype(np.float32), (P, 1))
    return c


def lay_out(inputs):
    a = {n: np.asarray(v) for n, v in inputs.items()}
    cols = np.concatenate([np.arange(416), np.arange(400, 416), np.arange(384, 400), np.arange(416, 2464)])
    column = lambda v: np.ascontiguousarray(v.reshape(-1, P).T)
    a["w_in"] = np.ascontiguousarray(a["w_in"][0][:, cols])
    for n in ("q_norm_g", "kv_norm_g", "hg_norm_g"):
        a[n] = column(a[n][0])
    a["mla_out_g"] = column(a["mla_out_g"][0])
    a["w_router"] = np.concatenate([a["w_router_group"][0], a["w_router_expert"][0]], axis=1)
    a["b_router"] = np.concatenate([a["b_router_group"], a["b_router_expert"]], axis=1)
    w = a["w_uq"][0].reshape(Q_RANK, HEADS, NOPE + ROPE)
    w = w[:, :, np.concatenate([np.arange(96), np.arange(80, 96), np.arange(64, 80)])]
    a["w_uq"] = np.ascontiguousarray(w.reshape(Q_RANK, HEADS // 2, 2, P).transpose(1, 0, 2, 3))
    w = a["w_ukv"][0].reshape(KV_RANK, HEADS // 2, 2, 2, NOPE)
    a["w_ukv"] = np.ascontiguousarray(w.transpose(1, 3, 0, 2, 4))
    a["hg_lb_logits"] = np.ascontiguousarray(a["hg_lb_logits"].reshape(2, HG, P).transpose(2, 0, 1))
    return a


def phase_0(nc, t, d):
    with ExitStack() as ctx:
        sb = lambda name, shape, dt=F32: ctx.enter_context(nc.sbuf_tensor(name, shape, dt))
        sem = lambda name: ctx.enter_context(nc.semaphore(name))
        pos_i = sb("pos_i", [P, SEQ], I32)
        ang = sb("ang", [P, SEQ])
        turns = sb("turns", [P, SEQ])
        lbl = sb("lbl", [P, 2, HG])
        lbm = sb("lbm", [P, HG])
        lbe = sb("lbe", [P, 2, HG])
        lbs = sb("lbs", [P, HG])
        loaded = sem("const_loaded")
        steps = sem("dve0_steps")
        act_steps = sem("act0_steps")
        with nc.Block() as block:
            @block.sync
            def _(sp):
                sp.dma_start(pos_i[:], d["positions"].broadcast_to([P, SEQ])).then_inc(loaded, 16)
                for dst, src in (
                    (t["ident"][:], d["ident"]), (t["causal"][:], d["causal"]), (t["fold"][:], d["fold"]),
                    (t["cols"][:], d["cols"]), (t["restart"][:], d["restart"]),
                    (lbl[:], d["hg_lb_logits"]), (t["gq"][:], d["q_norm_g"]),
                    (t["gkv"][:], d["kv_norm_g"]), (t["ghg"][:], d["hg_norm_g"]),
                ):
                    sp.dma_start(dst, src).then_inc(loaded, 16)
                sp.dma_start(t["xt"][:], d["x"][0].rearrange("(s i p) n -> s p i n", p=P, i=2)[0]).then_inc(t["x_loaded"], 16)
                w = d["w_in"].rearrange("(k p) n -> p k n", p=P)
                for (lo, hi), sem_ in zip(W_PARTS, t["w_in_loaded"]):
                    sp.dma_start(t["wi"][:, :, lo:hi], w[:, :, lo:hi]).then_inc(sem_, 16)
                sp.wait_ge(loaded, 160)

            @block.scalar
            def _(act):
                act.wait_ge(steps, 6)
                nc.scalar.activation(lbe[:], lbl[:], ACT.Exp).then_inc(act_steps, 1)
                act.wait_ge(steps, 15)
                nc.scalar.activation(t["trig"][:], ang[:], ACT.Sin).then_inc(act_steps, 1)

            @block.vector
            def _(v):
                n = [0]

                def step(ins, after=True):
                    n[0] += 1
                    ins.then_inc(steps, 1)
                    v.wait_ge(steps, n[0])
                v.wait_ge(loaded, 160)
                step(v.tensor_copy(ang[:], pos_i[:]))
                step(v.memset(t["ones"][:], 1.0))
                step(v.memset(t["cell"][:], 0.0))
                step(v.tensor_tensor(lbm[:], lbl[:, 0, :], lbl[:, 1, :], ALU.max))
                step(v.tensor_tensor(lbl[:, 0, :], lbl[:, 0, :], lbm[:], ALU.subtract))
                step(v.tensor_tensor(lbl[:, 1, :], lbl[:, 1, :], lbm[:], ALU.subtract))
                col = lambda c: t["cols"][:, c:c + 1]
                step(v.tensor_scalar(ang[:], ang[:], col(C_INVF), None, ALU.mult))
                step(v.tensor_scalar(turns[:], ang[:], 1.0 / (2 * np.pi), col(C_TURN), ALU.mult, ALU.add))
                step(v.tensor_scalar(turns[:], turns[:], ROUND, None, ALU.add))
                step(v.tensor_scalar(turns[:], turns[:], -ROUND, None, ALU.add))
                for part in (PI2_A, PI2_B, PI2_C):
                    step(v.scalar_tensor_tensor(ang[:], turns[:], -part, ang[:], ALU.mult, ALU.add))
                step(v.tensor_scalar(ang[:], ang[:], col(C_RAD), None, ALU.add))
                step(v.tensor_scalar(ang[:], ang[:], 3.1415925, -3.1415925, ALU.min, ALU.max))
                v.wait_ge(act_steps, 1)
                step(v.tensor_tensor(lbs[:], lbe[:, 0, :], lbe[:, 1, :], ALU.add))
                step(v.reciprocal(lbs[:], lbs[:]))
                step(v.tensor_tensor(t["lb"][:], lbe[:, 0, :], lbs[:], ALU.mult))
                step(v.tensor_scalar(t["oml"][:], t["lb"][:], -1.0, 1.0, ALU.mult, ALU.add))
                step(v.tensor_scalar(t["noml"][:], t["oml"][:], -1.0, None, ALU.mult))
                v.wait_ge(act_steps, 2)
                step(v.tensor_scalar(t["trig"][:], t["trig"][:], col(C_SIGN), None, ALU.mult))


def phase_a(nc, t, d):
    with ExitStack() as ctx:
        sb = lambda name, shape, dt=F32: ctx.enter_context(nc.sbuf_tensor(name, shape, dt))
        sems = []

        def sem(name):
            sems.append(nc.alloc_semaphore(name))
            return sems[-1]
        psum = lambda name: ctx.enter_context(nc.psum_tensor(name, [P, 512], F32))
        wi = t["wi"]
        xt, x_loaded = t["xt"], t["x_loaded"]
        xT = sb("xT", [P, KT, SPAN])
        gate = sb("gate", [P, HG, SPAN])
        key = sb("key", [P, HG, SPAN])
        logf = sb("logf", [P, HG, SPAN])
        ep = sb("ep", [P, HG, SPAN])
        en = sb("en", [P, HG, SPAN])
        qry = sb("qry", [P, HG, SPAN])
        gin = sb("gin", [P, HG, SPAN])
        sig = sb("sig", [P, HG, SPAN])
        ot = sb("ot", [P, HG, SPAN])
        rs = sb("rs", [P, HG, SPAN])
        vt = sb("vt", [P, 2, D_HG])
        kt = sb("kt", [P, 2, HG, P])
        am = sb("am", [P, 2, HG, P])
        state = sb("state", [P, 2, HG, P])
        lmx = sb("lmx", [P, HG, NC + 1])
        gsum = sb("gsum", [P, HG, NC])
        gsum2 = sb("gsum2", [P, HG, NC])
        gf = sb("gf", [P, HG, NC])
        cqr = sb("cqr", [P, 3, SPAN])
        csq = sb("csq", [P, 3, SPAN])
        crs = sb("crs", [P, 2, SPAN])

        B = [psum(f"pa{i}") for i in range(4)]
        OB = [psum("po0"), psum("po1")]
        UB = [psum("pu0"), psum("pu1")]

        x_turned = sem("x_turned")
        xT_act = sem("xT_act"); xT_dve = sem("xT_dve"); projected = sem("projected")
        f_exp = sem("f_exp"); v_ready = sem("v_ready"); q_ready = sem("q_ready")
        g_raw = sem("g_raw"); g_exp = sem("g_exp"); c_raw = sem("c_raw"); c_sq = sem("c_sq"); kr_ready = sem("kr_ready")
        sig_f = sem("sig_f"); key_ready = sem("key_ready"); logf_ready = sem("logf_ready")
        cum = sem("cum"); carry = sem("carry"); gsum_ready = sem("gsum_ready"); gf_ready = sem("gf_ready"); centred = sem("centred")
        ep_ready = sem("ep_ready"); en_ready = sem("en_ready"); scaled = sem("scaled"); init = sem("a_init")
        k_turned = sem("k_turned"); kt_ready = sem("kt_ready"); a_done = sem("a_done"); a_ready = sem("a_ready")
        u_done = sem("u_done"); state_ready = sem("state_ready"); inter_done = sem("inter_done")
        o_ready = sem("o_ready"); osq = sem("osq"); o_sum = sem("o_sum"); o_root = sem("o_root"); c_sum = sem("c_sum"); c_root = sem("c_root")
        silu = sem("silu"); r_steps = sem("r_steps"); c_steps = sem("c_steps"); stored = sem("r_stored")

        xd = d["x"][0].rearrange("(s i p) n -> s p i n", p=P, i=2)
        rT = d["rT"].rearrange("(h p) n -> p h n", p=P)

        with nc.Block() as block:
            @block.sync
            def _(sp):
                def span(m, last):
                    if not last:
                        sp.wait_ge(x_turned, m * 4 + 4)
                        sp.dma_start(xt[:], xd[m + 1]).then_inc(x_loaded, 16)
                    sp.wait_ge(r_steps, m * 3 + 3)
                    sp.dma_start(rT[:, :, bass.ds(m * SPAN, SPAN)], ot[:]).then_inc(stored, 16)
                span(0, False)
                with sp.Fori(1, NS - 1) as m:
                    span(m, False)
                span(NS - 1, True)
                sp.wait_ge(stored, 16 * NS)

            @block.tensor
            def _(pe):
                def turn_x(m):
                    pe.wait_ge(x_loaded, m * 16 + 16)
                    for n, b in enumerate((2, 3, 0, 1)):
                        for kk in range(2):
                            k = 2 * n + kk
                            for i in range(2):
                                ins = pe.transpose(B[b][:, kk * SPAN + i * P:kk * SPAN + (i + 1) * P],
                                                   xt[:, i, k * P:(k + 1) * P], t["ident"][:])
                        ins.then_inc(x_turned, 1)
                        yield n

                def project(b, col, m_cols):
                    for k in range(KT):
                        ins = pe.matmul(B[b][0:m_cols, 0:SPAN], wi[:, k, col:col + m_cols], xT[:, k, :],
                                        start=(k == 0), stop=(k == KT - 1))
                    ins.then_inc(projected, 1)

                def project_f(step):
                    h, part = divmod(step, 4)
                    for k in range(part * KT // 4, (part + 1) * KT // 4):
                        ins = pe.matmul(B[2 + h // 2][:, h % 2 * SPAN:(h % 2 + 1) * SPAN], wi[:, k, W_F + h * P:W_F + (h + 1) * P],
                                        xT[:, k, :], start=(k == 0), stop=(k == KT - 1))
                    if part == 3:
                        ins.then_inc(projected, 1)

                for _ in turn_x(0):
                    pass
                pe.wait_ge(t["w_in_loaded"][0], 16)
                pe.wait_ge(xT_act, 2)
                pe.wait_ge(xT_dve, 2)
                for step in range(16):
                    project_f(step)

                def span(m, last):
                    def weights(part):
                        if isinstance(m, int) and m == 0:
                            pe.wait_ge(t["w_in_loaded"][part], 16)
                    weights(1)
                    for i in range(2):
                        for k in range(KT):
                            ins = pe.matmul(B[i][:], xT[:, k, i * P:(i + 1) * P], wi[:, k, W_I:W_I + D_HG],
                                            start=(k == 0), stop=(k == KT - 1))
                        ins.then_inc(projected, 1)
                    weights(2)
                    for h in range(HG):
                        if h < 2:
                            pe.wait_ge(f_exp, m * 4 + 2 + 2 * h)
                        else:
                            pe.wait_ge(v_ready, m * 2 + h - 1)
                        project((2 + h) % 4, W_Q + h * P, P)
                    weights(3)
                    for h in range(HG):
                        pe.wait_ge(q_ready, m * 4 + 1 + h)
                        project((2 + h) % 4, W_G + h * P, P)
                    weights(4)
                    pe.wait_ge(g_exp, m * 4 + 1)
                    project(2, W_CKV, P)
                    pe.wait_ge(g_exp, m * 4 + 2)
                    project(3, W_KR, 64)
                    pe.wait_ge(g_exp, m * 4 + 3)
                    project(0, W_CQ, P)
                    pe.wait_ge(g_exp, m * 4 + 4)
                    project(1, W_CQ + P, P)
                    if not last:
                        turning = turn_x(m + 1)
                        pe.wait_ge(c_raw, m * 3 + 1)
                        pe.wait_ge(c_sq, m * 3 + 1)
                        next(turning)
                        pe.wait_ge(kr_ready, m + 1)
                        next(turning)
                        pe.wait_ge(c_raw, m * 3 + 2)
                        pe.wait_ge(c_sq, m * 3 + 2)
                        next(turning)
                        pe.wait_ge(c_raw, m * 3 + 3)
                        pe.wait_ge(c_sq, m * 3 + 3)
                        next(turning)
                    else:
                        pe.wait_ge(c_sq, m * 3 + 3)
                        pe.wait_ge(c_raw, m * 3 + 3)
                        pe.wait_ge(kr_ready, m + 1)
                    since(pe, o_root, m * 2)
                    for n, (lo, hi) in enumerate(((1, 3), (0, 1))):
                        for j in range(lo, hi):
                            ins = pe.matmul(UB[0][:, n * SPAN:(n + 1) * SPAN], t["ones"][:], csq[:, j, :],
                                            start=(j == lo), stop=(j == hi - 1))
                    ins.then_inc(c_sum, 1)
                    pe.wait_ge(scaled, m * 3 + 3)
                    for i in range(2):
                        if not last:
                            pe.wait_ge(xT_dve if i else xT_act, m * 2 + 3)
                        for h in range(HG):
                            ins = pe.matmul(B[2 + i][:, h * P:(h + 1) * P], key[:, h, i * P:(i + 1) * P],
                                            ep[:, h, i * P:(i + 1) * P], start=True, stop=True)
                        ins.then_inc(a_done, 1)
                    for i in range(2):
                        if not last:
                            pe.wait_ge(xT_dve if i else xT_act, m * 2 + 4)
                        for h in range(HG):
                            ins = pe.transpose(B[i][:, h * P:(h + 1) * P], key[:, h, i * P:(i + 1) * P], t["ident"][:])
                        ins.then_inc(k_turned, 1)
                    if not last:
                        pe.wait_ge(a_ready, m * 2 + 2)
                        project_f(0)
                    pe.wait_ge(kt_ready, m * 2 + 2)
                    pe.wait_ge(c_root, m * 2 + 2)

                    def update(c):
                        i, j = divmod(c, P // C)
                        if c >= 2:
                            pe.wait_ge(state_ready, m * NC + c - 1)
                        for h in range(HG):
                            ins = pe.matmul(UB[c % 2][:, h * P:(h + 1) * P], kt[j * C:(j + 1) * C, i, h, :],
                                            vt[j * C:(j + 1) * C, i, h * P:(h + 1) * P], start=True, stop=True,
                                            tile_position=(j * C, 0))
                        ins.then_inc(u_done, 1)

                    def inter(c):
                        i, j = divmod(c, P // C)
                        pe.wait_ge(state_ready, m * NC + c)
                        for h in range(HG):
                            ins = pe.matmul(OB[i][:, h * P + j * C:h * P + (j + 1) * C], state[:, (c + 1) % 2, h, :],
                                            qry[:, h, i * P + j * C:i * P + (j + 1) * C],
                                            start=False, stop=True, skip_group_check=True)
                        ins.then_inc(inter_done, 1)

                    update(0)
                    update(1)
                    for c in range(NC):
                        i, j = divmod(c, P // C)
                        if j == 0:
                            pe.wait_ge(a_ready, m * 2 + 1 + i)
                            pe.wait_ge(osq, m * 2 + i)
                            for h in range(HG):
                                pe.matmul(OB[i][:, h * P:(h + 1) * P], vt[:, i, h * P:(h + 1) * P], am[:, i, h, :],
                                          start=(h == 0), stop=False, skip_group_check=True)
                        inter(c)
                        if c + 2 < NC:
                            update(c + 2)
                        if not last:
                            for step in range(2 * c + 1, min(2 * c + 3, 16)):
                                project_f(step)
                    pe.wait_ge(osq, m * 2 + 2)
                    pe.wait_ge(state_ready, m * NC + NC)
                    for n in range(2):
                        pe.matmul(UB[n][:], t["ones"][:], en[:, 2 * n:2 * n + 2, :], start=True, stop=True).then_inc(o_sum, 1)
                span(0, False)
                with pe.Fori(1, NS - 1) as m:
                    span(m, False)
                span(NS - 1, True)

            @block.scalar
            def _(act):
                def xT_part(m):
                    for n in range(0, 4, 2):
                        act.wait_ge(x_turned, m * 4 + 1 + n)
                        nc.scalar.copy(xT[:, 2 * n:2 * n + 2, :], B[(2 + n) % 4][:].rearrange("p (k n) -> p k n", k=2)).then_inc(xT_act, 1)
                xT_part(0)

                def span(m, last):
                    since(act, scaled, m * 3)
                    since(act, key_ready, m * 4)
                    since(act, logf_ready, m * 4)
                    for h in range(HG):
                        act.wait_ge(projected, m * 18 + 2 + h // 2 * 2)
                        nc.scalar.activation(gate[:, h, :], B[2 + h // 2][:, h % 2 * SPAN:(h % 2 + 1) * SPAN], ACT.Exp, scale=-1.0).then_inc(f_exp, 1)
                    act.wait_ge(sig_f, m * 2 + 2)
                    since(act, r_steps, m * 3)
                    for h in range(HG):
                        nc.scalar.activation(logf[:, h, :], gate[:, h, :], ACT.Ln, bias=t["lb"][:, h:h + 1],
                                             scale=t["oml"][:, h:h + 1]).then_inc(logf_ready, 1)
                    since(act, k_turned, m * 2)
                    since(act, a_done, m * 2)
                    for h in range(HG):
                        nc.scalar.activation(key[:, h, :], gate[:, h, :], ACT.Identity, bias=t["oml"][:, h:h + 1],
                                             scale=t["noml"][:, h:h + 1]).then_inc(key_ready, 1)
                    act.wait_ge(gsum_ready, m + 1)
                    nc.scalar.activation(gf[:], gsum[:], ACT.Exp).then_inc(gf_ready, 1)
                    act.wait_ge(centred, m + 1)
                    since(act, a_done, m * 2)
                    nc.scalar.activation(ep[:], logf[:], ACT.Exp).then_inc(ep_ready, 1)
                    since(act, o_sum, m * 2)
                    nc.scalar.activation(en[:], logf[:], ACT.Exp, scale=-1.0).then_inc(en_ready, 1)
                    for h in range(HG):
                        act.wait_ge(projected, m * 18 + 11 + h)
                        b = B[(2 + h) % 4][:, 0:SPAN]
                        nc.scalar.copy(gin[:, h, :], b).then_inc(g_raw, 1)
                        nc.scalar.activation(sig[:, h, :], b, ACT.Exp, scale=-1.0).then_inc(g_exp, 1)
                    act.wait_ge(c_sum, m)
                    since(act, c_steps, m * 4)
                    for n, (p, b) in enumerate(((15, 2), (17, 0), (18, 1))):
                        act.wait_ge(projected, m * 18 + p)
                        nc.scalar.copy(cqr[:, n, :], B[b][:, 0:SPAN]).then_inc(c_raw, 1)
                        nc.scalar.square(csq[:, n, :], B[b][:, 0:SPAN]).then_inc(c_sq, 1)
                    if not last:
                        act.wait_ge(projected, m * 18 + 18)
                        xT_part(m + 1)
                    act.wait_ge(c_sum, m + 1)
                    since(act, c_steps, m * 4)
                    for n, rank in enumerate((Q_RANK, KV_RANK)):
                        nc.scalar.activation(crs[:, n, :], UB[0][:, n * SPAN:(n + 1) * SPAN], ACT.Sqrt, scale=1.0 / rank,
                                             bias=t["cols"][:, C_REPS:C_REPS + 1]).then_inc(c_root, 1)
                    for i in range(2):
                        act.wait_ge(k_turned, m * 2 + 1 + i)
                        nc.scalar.copy(kt[:, i], B[i][:].rearrange("p (h n) -> p h n", h=HG)).then_inc(kt_ready, 1)
                    since(act, stored, m * 16)
                    act.wait_ge(scaled, m * 3 + 3)
                    for i in range(2):
                        act.wait_ge(inter_done, m * NC + (i + 1) * NC // 2)
                        o = OB[i][:].rearrange("p (h n) -> p h n", h=HG)
                        nc.scalar.copy(ot[:, :, i * P:(i + 1) * P], o).then_inc(o_ready, 1)
                        nc.scalar.square(en[:, :, i * P:(i + 1) * P], o).then_inc(osq, 1)
                    for n in range(2):
                        act.wait_ge(o_sum, m * 2 + 1 + n)
                        nc.scalar.activation(rs[:, 2 * n:2 * n + 2, :], UB[n][:].rearrange("p (h n) -> p h n", h=2), ACT.Sqrt,
                                             scale=1.0 / DK, bias=t["cols"][:, C_REPS:C_REPS + 1]).then_inc(o_root, 1)
                span(0, False)
                with act.Fori(1, NS - 1) as m:
                    span(m, False)
                span(NS - 1, True)

            @block.gpsimd
            def _(pool):
                nc.gpsimd.memset(state[:, 1], 0.0).then_inc(init, 1)
                nc.gpsimd.memset(lmx[:, :, NC:NC + 1], 0.0).then_inc(init, 1)

            @block.vector
            def _(v):
                def xT_part(m):
                    for n in range(1, 4, 2):
                        v.wait_ge(x_turned, m * 4 + 1 + n)
                        v.tensor_copy(xT[:, 2 * n:2 * n + 2, :], B[(2 + n) % 4][:].rearrange("p (k n) -> p k n", k=2)).then_inc(xT_dve, 1)
                xT_part(0)
                v.wait_ge(init, 2)

                def span(m, last):
                    v.wait_ge(f_exp, m * 4 + 4)
                    v.tensor_scalar(gate[:], gate[:], 1.0, None, ALU.add).then_inc(sig_f, 1)
                    v.wait_ge(sig_f, m * 2 + 1)
                    v.reciprocal(gate[:], gate[:]).then_inc(sig_f, 1)
                    def values(i):
                        v.wait_ge(projected, m * 18 + 5 + i)
                        if i == 0:
                            since(v, inter_done, m * NC)
                        v.tensor_copy(vt[:, i, :], B[i][:]).then_inc(v_ready, 1)
                    values(0)
                    v.wait_ge(logf_ready, m * 4 + 4)
                    flat = logf[:].rearrange("p h n -> p (h n)")
                    v.tensor_tensor_scan(flat, t["restart"][:], flat, 0.0, ALU.mult, ALU.add).then_inc(cum, 1)
                    v.tensor_copy(lmx[:, :, 0:1], lmx[:, :, NC:NC + 1]).then_inc(carry, 1)
                    v.wait_ge(cum, m * 2 + 1)
                    v.wait_ge(carry, m * 2 + 1)
                    b4 = logf[:].rearrange("p h (c s) -> p h c s", s=C)
                    v.tensor_tensor(lmx[:, :, 1:NC + 1], b4[:, :, :, C - 1], b4[:, :, :, C // 2 - 1], ALU.subtract).then_inc(carry, 1)
                    v.wait_ge(carry, m * 2 + 2)
                    v.wait_ge(gf_ready, m)
                    v.tensor_tensor(gsum[:], b4[:, :, :, C // 2 - 1], lmx[:, :, 0:NC], ALU.add).then_inc(gsum_ready, 1)
                    v.wait_ge(gsum_ready, m + 1)
                    v.tensor_copy(gsum2[:], b4[:, :, :, C // 2 - 1]).then_inc(cum, 1)
                    v.wait_ge(cum, m * 2 + 2)
                    bc = logf[:].rearrange("p h (c s) -> p (h c) s", s=C)
                    mid = gsum2[:].rearrange("p h c -> p (h c)").unsqueeze(2).broadcast_to([P, HG * NC, C])
                    v.tensor_tensor(bc, bc, mid, ALU.subtract).then_inc(centred, 1)
                    values(1)
                    for h in range(HG):
                        v.wait_ge(projected, m * 18 + 7 + h)
                        v.tensor_copy(qry[:, h, :], B[(2 + h) % 4][:, 0:SPAN]).then_inc(q_ready, 1)
                    v.wait_ge(q_ready, m * 4 + 4)
                    v.wait_ge(ep_ready, m + 1)
                    v.tensor_tensor(ep[:], qry[:], ep[:], ALU.mult).then_inc(scaled, 1)
                    v.wait_ge(key_ready, m * 4 + 4)
                    v.wait_ge(en_ready, m + 1)
                    v.tensor_tensor(key[:], key[:], en[:], ALU.mult).then_inc(scaled, 1)
                    v.wait_ge(gf_ready, m + 1)
                    v.wait_ge(scaled, m * 3 + 1)
                    v.tensor_tensor(qry[:].rearrange("p h (c s) -> p (h c) s", s=C), ep[:].rearrange("p h (c s) -> p (h c) s", s=C),
                                    gf[:].rearrange("p h c -> p (h c)").unsqueeze(2).broadcast_to([P, HG * NC, C]),
                                    ALU.mult).then_inc(scaled, 1)
                    v.wait_ge(g_exp, m * 4 + 4)
                    v.tensor_scalar(sig[:], sig[:], 1.0, None, ALU.add).then_inc(silu, 1)
                    v.wait_ge(silu, m * 3 + 1)
                    v.reciprocal(sig[:], sig[:]).then_inc(silu, 1)
                    v.wait_ge(silu, m * 3 + 2)
                    v.wait_ge(g_raw, m * 4 + 4)
                    v.tensor_tensor(gin[:], gin[:], sig[:], ALU.mult).then_inc(silu, 1)
                    v.wait_ge(projected, m * 18 + 16)
                    v.tensor_tensor(t["krp"][0:64, bass.ds(m * SPAN, SPAN)], B[3][0:64, 0:SPAN],
                                    t["trig"][0:64, bass.ds(m * SPAN, SPAN)], ALU.mult).then_inc(kr_ready, 1)
                    if not last:
                        v.wait_ge(projected, m * 18 + 18)
                        xT_part(m + 1)
                    for i in range(2):
                        v.wait_ge(a_done, m * 2 + 1 + i)
                        v.scalar_tensor_tensor(am[:, i], B[2 + i][:].rearrange("p (h n) -> p h n", h=HG), 3.0e38,
                                               t["causal"][:].unsqueeze(1).broadcast_to([P, HG, P]),
                                               ALU.min, ALU.mult).then_inc(a_ready, 1)
                    for c in range(NC):
                        v.wait_ge(u_done, m * NC + 1 + c)
                        v.wait_ge(inter_done, m * NC + c)
                        v.wait_ge(state_ready, m * NC + c)
                        for h in range(HG):
                            ins = v.scalar_tensor_tensor(state[:, c % 2, h, :], state[:, (c + 1) % 2, h, :], gf[:, h, c:c + 1],
                                                         UB[c % 2][:, h * P:(h + 1) * P], ALU.mult, ALU.add)
                        ins.then_inc(state_ready, 1)
                    v.wait_ge(c_root, m * 2 + 2)
                    v.reciprocal(crs[:], crs[:]).then_inc(c_steps, 1)
                    v.wait_ge(c_steps, m * 4 + 1)
                    v.wait_ge(c_raw, m * 3 + 3)
                    for j in range(2):
                        v.scalar_tensor_tensor(t["cqn"][:, j, bass.ds(m * SPAN, SPAN)], cqr[:, 1 + j, :], t["gq"][:, j:j + 1],
                                               crs[:, 0, :], ALU.mult, ALU.mult).then_inc(c_steps, 1)
                    v.scalar_tensor_tensor(t["ckvn"][:, bass.ds(m * SPAN, SPAN)], cqr[:, 0, :], t["gkv"][:, 0:1],
                                           crs[:, 1, :], ALU.mult, ALU.mult).then_inc(c_steps, 1)
                    v.wait_ge(o_root, m * 2 + 2)
                    v.reciprocal(rs[:], rs[:]).then_inc(r_steps, 1)
                    v.wait_ge(r_steps, m * 3 + 1)
                    v.wait_ge(o_ready, m * 2 + 2)
                    v.scalar_tensor_tensor(ot[:], ot[:], t["ghg"][:, 0:1], rs[:], ALU.mult, ALU.mult).then_inc(r_steps, 1)
                    v.wait_ge(r_steps, m * 3 + 2)
                    v.wait_ge(silu, m * 3 + 3)
                    v.tensor_tensor(ot[:], ot[:], gin[:], ALU.mult).then_inc(r_steps, 1)
                span(0, False)
                with v.Fori(1, NS - 1) as m:
                    span(m, False)
                span(NS - 1, True)
        nc.clear_and_free_semaphores(sems)
        nc.all_engine_barrier()


QT_ORDER = [q for i in range(NT // 2) for q in (i, NT - 1 - i)]
ITEMS = [(x, q) for x in range(2) for q in QT_ORDER]
BANKS = [(q + 4) // 4 for _, q in ITEMS]
FIRST_BANK = [sum(BANKS[:n]) for n in range(len(ITEMS) + 1)]
NI, NBK = len(ITEMS), FIRST_BANK[len(ITEMS)]


def phase_b(nc, t, d):
    with ExitStack() as ctx:
        sb = lambda name, shape, dt=F32: ctx.enter_context(nc.sbuf_tensor(name, shape, dt))
        sem = lambda name: ctx.enter_context(nc.semaphore(name))
        psum = lambda name, n=512: ctx.enter_context(nc.psum_tensor(name, [P, n], F32))
        wq = sb("wq", [P, 2, 2, P])
        wk = sb("wk", [P, 2, NOPE])
        wv = sb("wv", [P, 2, VD])
        qT = sb("qT", [P, 2, SEQ])
        kT = sb("kT", [P, 2, SEQ])
        vp = sb("vp", [P, NT, 2 * VD])
        pr = sb("pr", [P, 2, SEQ])
        prT = sb("prT", [P, 2, NT, P])
        mx = sb("mx", [P, NI, 4])
        mxa = sb("mxa", [P, NI])
        nmx = sb("nmx", [P, NI])
        rsum = sb("rsum", [P, NI, 4])
        rsa = sb("rsa", [P, NI])
        rin = sb("rin", [P, NI])
        S = [psum(f"pS{i}") for i in range(4)]
        TB = [psum(f"pT{i}") for i in range(2)]
        OB = [psum(f"pO{i}") for i in range(2)]
        w_loaded = sem("w_loaded"); folded = sem("folded"); rope_copied = sem("rope_copied")
        prep = sem("prep"); prep_act = sem("prep_act"); prep_dve = sem("prep_dve")
        s_done = sem("s_done"); masked = sem("masked"); mx_part = sem("mx_part"); mx_all = sem("mx_all"); nmx_ready = sem("nmx_ready")
        exp_done = sem("exp_done"); t_done = sem("t_done"); t_dve = sem("t_dve"); t_act = sem("t_act")
        pv_done = sem("pv_done"); rs_ready = sem("rs_ready"); rin_ready = sem("rin_ready"); o_out = sem("o_out")
        wq_d = d["w_uq"].rearrange("g (k p) x c -> g p k x c", p=P)
        wkv_d = d["w_ukv"]
        PREP = [("k", x, c) for x in range(2) for c in range(4)] + [("q", x, c) for x in range(2) for c in range(4)] + \
               [("v", 0, c) for c in range(4)]
        NP = len(PREP)

        def pairs(eng, pair):
            pair(0)
            with eng.Fori(1, HEADS // 2) as g:
                pair(g)

        with nc.Block() as block:
            @block.sync
            def _(sp):
                def weights(g):
                    if not isinstance(g, int) or g > 0:
                        since(sp, prep, g * NP)
                    sp.dma_start(wq[:], wq_d[g]).then_inc(w_loaded, 16)
                    sp.dma_start(wk[:], wkv_d[g, 0]).then_inc(w_loaded, 16)
                    sp.dma_start(wv[:], wkv_d[g, 1]).then_inc(w_loaded, 16)
                weights(0)
                for name, src in (("ga", d["mla_out_g"]), ("wr", d["w_router"].rearrange("(k p) n -> p k n", p=P)),
                                  ("rb", d["b_router"].broadcast_to([P, NG + NE])), ("g1", d["ln1_g"].broadcast_to([P, DM])),
                                  ("b1", d["ln1_b"].broadcast_to([P, DM]))):
                    sp.dma_start(t[name][:], src).then_inc(t["c_loaded"], 16)
                with sp.Fori(1, HEADS // 2) as g:
                    weights(g)

            @block.tensor
            def _(pe):
                for c in range(4):
                    ins = pe.matmul(S[c][64:128, :], t["fold"][0:64, 64:128], t["krp"][0:64, c * 512:(c + 1) * 512],
                                    start=True, stop=True, tile_position=(0, 64))
                    ins.then_inc(folded, 1)

                def pair(g):
                    pe.wait_ge(w_loaded, g * 48 + 48)
                    since(pe, exp_done, g * NBK)
                    pe.wait_ge(rope_copied, 8)
                    for n, (kind, x, c) in enumerate(PREP):
                        if n >= 4:
                            pe.wait_ge(prep_act, g * NP + n - 3)
                        if n >= 12:
                            pe.wait_ge(prep_dve, g * 8 + min(n - 4 - 8 + 1, 8))
                        b = S[n % 4]
                        if kind == "k":
                            ins = pe.matmul(b[0:64, :], wk[:, x, :], t["ckvn"][:, c * 512:(c + 1) * 512], start=True, stop=True)
                        elif kind == "q":
                            for k in range(2):
                                ins = pe.matmul(b[:], wq[:, k, x, :], t["cqn"][:, k, c * 512:(c + 1) * 512],
                                                start=(k == 0), stop=(k == 1))
                        else:
                            for i in range(4):
                                ins = pe.matmul(b[:, i * P:(i + 1) * P], t["ckvn"][:, (4 * c + i) * P:(4 * c + i + 1) * P],
                                                wv[:].rearrange("p x c -> p (x c)"), start=True, stop=True)
                        ins.then_inc(prep, 1)
                    pe.wait_ge(prep_act, g * NP + NP)
                    pe.wait_ge(prep_dve, g * 8 + 8)

                    def turn(n, gr):
                        x, q = ITEMS[n]
                        u = FIRST_BANK[n] + gr
                        if gr == 0:
                            pe.wait_ge(exp_done, g * NBK + FIRST_BANK[n + 1])
                        if u >= 2:
                            pe.wait_ge(t_dve if u % 2 == 0 else t_act, g * (NBK // 2) + u // 2)
                        for i in range(min(4, q + 1 - 4 * gr)):
                            kt_ = 4 * gr + i
                            ins = pe.transpose(TB[u % 2][:, i * P:(i + 1) * P], pr[:, n % 2, kt_ * P:(kt_ + 1) * P], t["ident"][:])
                        ins.then_inc(t_done, 1)

                    def weigh(n, gr):
                        x, q = ITEMS[n]
                        u = FIRST_BANK[n] + gr
                        if gr == 0 and n >= 2:
                            pe.wait_ge(o_out, g * NI + n - 1)
                        pe.wait_ge(t_dve if u % 2 == 0 else t_act, g * (NBK // 2) + u // 2 + 1)
                        for i in range(min(4, q + 1 - 4 * gr)):
                            kt_ = 4 * gr + i
                            ins = pe.matmul(OB[n % 2][:, 0:VD], prT[:, n % 2, kt_, :], vp[:, kt_, x * VD:(x + 1) * VD],
                                            start=(kt_ == 0), stop=(kt_ == q))
                        if gr == BANKS[n] - 1:
                            ins.then_inc(pv_done, 1)

                    since(pe, o_out, g * NI)
                    since(pe, t_dve, g * (NBK // 2))
                    since(pe, t_act, g * (NBK // 2))
                    for n in range(NI + 2):
                        if n < NI:
                            x, q = ITEMS[n]
                            for j in range(BANKS[n]):
                                u = FIRST_BANK[n] + j
                                if u >= 4:
                                    pe.wait_ge(exp_done, g * NBK + u - 3)
                                w = min(512, (q + 1) * P - j * 512)
                                pe.matmul(S[u % 4][:, 0:w], qT[:, x, q * P:(q + 1) * P], kT[:, x, j * 512:j * 512 + w],
                                          start=True, stop=True).then_inc(s_done, 1)
                        turns = BANKS[n - 1] if 1 <= n <= NI else 0
                        weighs = BANKS[n - 2] if n >= 2 else 0
                        for gr in range(4):
                            if gr < turns:
                                turn(n - 1, gr)
                            if gr < weighs:
                                weigh(n - 2, gr)
                pairs(pe, pair)

            @block.scalar
            def _(act):
                for c in range(4):
                    act.wait_ge(folded, c + 1)
                    for x in range(2):
                        nc.scalar.copy(kT[64:128, x, c * 512:(c + 1) * 512], S[c][64:128, :]).then_inc(rope_copied, 1)

                def pair(g):
                    since(act, pv_done, g * NI)
                    for n, (kind, x, c) in enumerate(PREP):
                        act.wait_ge(prep, g * NP + n + 1)
                        b = S[n % 4]
                        if kind == "k":
                            ins = nc.scalar.copy(kT[0:64, x, c * 512:(c + 1) * 512], b[0:64, :])
                        elif kind == "q":
                            ins = nc.scalar.copy(qT[0:64, x, c * 512:(c + 1) * 512], b[0:64, :])
                        else:
                            ins = nc.scalar.copy(vp[:, 4 * c:4 * c + 4, :], b[:].rearrange("p (i c) -> p i c", i=4))
                        ins.then_inc(prep_act, 1)
                    for n in range(NI + 1):
                        if n < NI:
                            x, q = ITEMS[n]
                            if n >= 2:
                                act.wait_ge(t_done, g * NBK + FIRST_BANK[n - 1])
                            act.wait_ge(nmx_ready, g * NI + n + 1)
                            for j in range(BANKS[n]):
                                u = FIRST_BANK[n] + j
                                w = min(512, (q + 1) * P - j * 512)
                                nc.scalar.activation(pr[:, n % 2, j * 512:j * 512 + w], S[u % 4][:, 0:w], ACT.Exp, scale=SCALE,
                                                     bias=nmx[:, n:n + 1], accum_out=rsum[:, n, j:j + 1]).then_inc(exp_done, 1)
                        if n >= 1:
                            m = n - 1
                            for gr in range(BANKS[m]):
                                u = FIRST_BANK[m] + gr
                                if u % 2 == 1:
                                    w = min(4, ITEMS[m][1] + 1 - 4 * gr)
                                    act.wait_ge(t_done, g * NBK + u + 1)
                                    if m >= 2:
                                        act.wait_ge(pv_done, g * NI + m - 1)
                                    nc.scalar.copy(prT[:, m % 2, 4 * gr:4 * gr + w, :],
                                                   TB[1][:, 0:w * P].rearrange("p (i c) -> p i c", i=w)).then_inc(t_act, 1)
                pairs(act, pair)

            @block.vector
            def _(v):
                def pair(g):
                    since(v, pv_done, g * NI)
                    for n, (kind, x, c) in enumerate(PREP):
                        if kind == "q":
                            v.wait_ge(prep, g * NP + n + 1)
                            v.tensor_tensor(qT[64:128, x, c * 512:(c + 1) * 512], S[n % 4][64:128, :],
                                            t["trig"][64:128, c * 512:(c + 1) * 512], ALU.mult).then_inc(prep_dve, 1)
                    for n in range(NI + 2):
                        if n < NI:
                            x, q = ITEMS[n]
                            nb = BANKS[n]
                            since(v, exp_done, g * NBK)
                            for j in range(nb):
                                u = FIRST_BANK[n] + j
                                w = min(512, (q + 1) * P - j * 512)
                                v.wait_ge(s_done, g * NBK + u + 1)
                                if j == nb - 1:
                                    v.memset(S[u % 4][0:64, w - 64:w], -3.0e38).then_inc(masked, 1)
                                    v.wait_ge(masked, g * NI + n + 1)
                                v.tensor_reduce(mx[:, n, j:j + 1], S[u % 4][:, 0:w], AX, ALU.max).then_inc(mx_part, 1)
                            v.wait_ge(mx_part, g * NBK + FIRST_BANK[n + 1])
                            v.tensor_reduce(mxa[:, n:n + 1], mx[:, n, 0:nb], AX, ALU.max).then_inc(mx_all, 1)
                            v.wait_ge(mx_all, g * NI + n + 1)
                            v.tensor_scalar(nmx[:, n:n + 1], mxa[:, n:n + 1], -SCALE, None, ALU.mult).then_inc(nmx_ready, 1)
                        if 1 <= n <= NI:
                            m = n - 1
                            for gr in range(BANKS[m]):
                                u = FIRST_BANK[m] + gr
                                if u % 2 == 0:
                                    w = min(4, ITEMS[m][1] + 1 - 4 * gr)
                                    v.wait_ge(t_done, g * NBK + u + 1)
                                    if m >= 2:
                                        v.wait_ge(pv_done, g * NI + m - 1)
                                    v.tensor_copy(prT[:, m % 2, 4 * gr:4 * gr + w, :],
                                                  TB[0][:, 0:w * P].rearrange("p (i c) -> p i c", i=w)).then_inc(t_dve, 1)
                        if n >= 2:
                            m = n - 2
                            x, q = ITEMS[m]
                            v.wait_ge(exp_done, g * NBK + FIRST_BANK[m + 1])
                            v.tensor_reduce(rsa[:, m:m + 1], rsum[:, m, 0:BANKS[m]], AX, ALU.add).then_inc(rs_ready, 1)
                            v.wait_ge(rs_ready, g * NI + m + 1)
                            v.reciprocal(rin[:, m:m + 1], rsa[:, m:m + 1]).then_inc(rin_ready, 1)
                            v.wait_ge(pv_done, g * NI + m + 1)
                            v.wait_ge(rin_ready, g * NI + m + 1)
                            v.tensor_scalar(t["ao"][:, q, bass.ds(g * (2 * VD) + x * VD, VD)], OB[m % 2][:, 0:VD],
                                            rin[:, m:m + 1], None, ALU.mult).then_inc(o_out, 1)
                pairs(v, pair)


def phase_c(nc, t, d):
    with ExitStack() as ctx:
        sb = lambda name, shape, dt=F32: ctx.enter_context(nc.sbuf_tensor(name, shape, dt))
        sem = lambda name: ctx.enter_context(nc.semaphore(name))
        psum = lambda name, n=512: ctx.enter_context(nc.psum_tensor(name, [P, n], F32))
        wr, rb, ga, g1, b1 = (t[n] for n in ("wr", "rb", "ga", "g1", "b1"))
        c_loaded = t["c_loaded"]
        wh = sb("wo_hi", [P, KT, DM], F32R); wl = sb("wo_lo", [P, KT, DM], F32R)
        rts = sb("rts", [P, 4, 2 * P])
        rh = sb("rts_hi", [P, 2, 4, P], F32R); rl = sb("rts_lo", [P, 2, 4, P], F32R)
        xs = sb("xs", [P, 2, DM])
        ap = sb("ap", [P, 2, 512])
        ass = sb("ass", [P, 2])
        ars = sb("ars", [P, 2])
        an = sb("an", [P, 2, 512])
        ah = sb("anT_hi", [P, 2, 4, P], F32R); al = sb("anT_lo", [P, 2, 4, P], F32R)
        hp = sb("hp", [P, 2, DM])
        st = sb("st", [P, 2, 2, 6])
        mv = sb("mv", [P, 2, 2])
        sd = sb("sd", [P, 2])
        rstd = sb("rstd", [P, 2])
        hT = sb("hT", [P, 2, KT, P])
        A = [psum(f"cA{i}") for i in range(1)]
        M = [psum(f"cM{i}") for i in range(4)]
        H = [psum(f"cH{i}") for i in range(2)]
        L = psum("cL")
        r_loaded = sem("r_loaded"); x_loaded = sem("xc_loaded")
        a_picked = sem("a_picked"); a_sum = sem("a_sum"); a_root = sem("a_root"); a_rs = sem("a_rs"); a_norm = sem("a_norm"); a_turned = sem("a_turned"); ah_ready = sem("ah_ready"); al_ready = sem("al_ready"); rh_ready = sem("rh_ready"); rl_ready = sem("rl_ready"); wh_ready = sem("wh_ready"); wl_ready = sem("wl_ready")
        mixed = sem("mixed"); res = sem("res"); stats = sem("stats"); aggr = sem("aggr"); root = sem("root"); rstd_ready = sem("rstd_ready")
        normed = sem("normed"); h_steps = sem("h_steps"); h_ready = sem("h_ready"); stored = [sem("h_stored0"), sem("h_stored1")]
        h_turned = sem("h_turned"); hT_dve = sem("hT_dve"); hT_act = sem("hT_act"); l_done = sem("l_done"); l_ready = sem("l_ready")
        rT = d["rT"].rearrange("(h p) n -> p h n", p=P)
        xd = d["x"][0].rearrange("(s i p) n -> s p i n", p=P, i=2)
        hd = d["h"].rearrange("(s i p) n -> s i p n", p=P, i=2)
        STEPS = NT // 2
        held = sem("hold_c")
        W_ORDER = (4, 5, 6, 7, 0, 1, 2, 3)
        w_loaded = [sem(f"wo_loaded{i}") for i in range(4)]

        def words(n):
            return hp[:, n % 4] if n % 4 < 2 else hT[:, n % 4 - 2].rearrange("p k n -> p (k n)")

        def steps(eng, step):
            step(0, True, False)
            with eng.Fori(1, STEPS - 1) as m:
                step(m, False, False)
            step(STEPS - 1, False, True)

        with nc.Block() as block:
            @block.sync
            def _(sp):
                sp.dma_start(rts[:], rT[:, :, 0:2 * P]).then_inc(r_loaded, 16)
                w = d["w_out"][0].rearrange("(k p) n -> p k n", p=P)
                for n, k in enumerate(W_ORDER):
                    if n >= 4:
                        sp.wait_ge(wl_ready, n - 3)
                    sp.dma_start(words(n), w[:, k]).then_inc(w_loaded[n % 4], 16)
                sp.dma_start(xs[:], xd[0]).then_inc(x_loaded, 16)

                def step(m, last):
                    for i in range(2):
                        if i == 1 and not last:
                            sp.wait_ge(rl_ready, m * 2 + 2)
                            sp.dma_start(rts[:], rT[:, :, bass.ds((m + 1) * 2 * P, 2 * P)]).then_inc(r_loaded, 16)
                            sp.wait_ge(res, m * 4 + 4)
                            sp.dma_start(xs[:], xd[m + 1]).then_inc(x_loaded, 16)
                        sp.wait_ge(h_ready, m * 2 + 1 + i)
                        sp.dma_start(hd[m, i], hp[:, i]).then_inc(stored[i], 16)
                with sp.Fori(0, STEPS - 1) as m:
                    step(m, False)
                step(STEPS - 1, True)
                for i in range(2):
                    sp.wait_ge(stored[i], 16 * STEPS)

            @block.tensor
            def _(pe):
                def project(m, i):
                    if i > 0 or not isinstance(m, int) or m > 0:
                        pe.wait_ge(res, m * 4 + 2 * i - 2)
                    for part in (1, 0):
                        if i == 0 and isinstance(m, int) and m == 0:
                            pe.wait_ge(wl_ready, 8 - 4 * part)
                        hi, lo = (ah, al) if part == 0 else (rh, rl)
                        pe.wait_ge(ah_ready if part == 0 else rh_ready, m * 2 + i + 1)
                        pe.wait_ge(al_ready if part == 0 else rl_ready, m * 2 + i + 1)
                        for half in range(2):
                            at = slice(half * 512, (half + 1) * 512)
                            for k in range(4):
                                w = wh[:, 4 * part + k, at], wl[:, 4 * part + k, at]
                                for n, (x, y) in enumerate(((hi, w[0]), (lo, w[0]), (hi, w[1]))):
                                    ins = pe.matmul(M[2 * i + half][:], x[:, i, k, :], y, start=(part == 1 and k == 0 and n == 0),
                                                    stop=(part == 0 and k == 3 and n == 2))
                        if part == 1 and i == 0:
                            turn_a(m, 1)
                    ins.then_inc(mixed, 1)

                def turn_a(m, i):
                    pe.wait_ge(a_norm, m * 2 + i + 1)
                    if i > 0 or not isinstance(m, int) or m > 0:
                        pe.wait_ge(ah_ready, m * 2 + i)
                        pe.wait_ge(al_ready, m * 2 + i)
                    for k in range(4):
                        ins = pe.transpose(A[0][:, k * P:(k + 1) * P], an[:, i, k * P:(k + 1) * P], t["ident"][:])
                    ins.then_inc(a_turned, 1)

                def route(n, i):
                    pe.wait_ge(h_ready, n + 1)
                    pe.wait_ge(hT_dve, n)
                    pe.wait_ge(hT_act, n)
                    for half in range(2):
                        for k in range(4):
                            ins = pe.transpose(H[half][:, k * P:(k + 1) * P], hp[:, i, (4 * half + k) * P:(4 * half + k + 1) * P], t["ident"][:])
                        ins.then_inc(h_turned, 1)

                def logits(n, i):
                    pe.wait_ge(hT_dve, n + 1)
                    pe.wait_ge(hT_act, n + 1)
                    pe.wait_ge(l_ready, n + 1)
                    for k in range(KT):
                        ins = pe.matmul(L[:, 0:NG + NE], hT[:, i, k, :], wr[:, k, :], start=(k == 0), stop=(k == KT - 1))
                    ins.then_inc(l_done, 1)

                def step(m, first):
                    turn_a(m, 0)
                    project(m, 0)
                    if not first:
                        logits(m * 2 - 2, 0)
                        route(m * 2 - 1, 1)
                    project(m, 1)
                    if not first:
                        logits(m * 2 - 1, 1)
                    route(m * 2, 0)
                pe.wait_ge(c_loaded, 5 * 16)
                step(0, True)
                with pe.Fori(1, STEPS) as m:
                    step(m, False)
                logits(NT - 2, 0)
                route(NT - 1, 1)
                logits(NT - 1, 1)

            @block.scalar
            def _(act):
                act.wait_ge(c_loaded, 5 * 16)
                def split_r(m, i):
                    act.wait_ge(r_loaded, m * 16 + 16)
                    if not isinstance(m, int) or m > 0:
                        act.wait_ge(mixed, m * 2 + i - 1)
                    nc.scalar.copy(rh[:, i], rts[:, :, i * P:(i + 1) * P]).then_inc(rh_ready, 1)

                def turned(n, i):
                    act.wait_ge(h_turned, 2 * n + 2)
                    act.wait_ge(l_done, n)
                    nc.scalar.copy(hT[:, i, 4:8, :], H[1][:].rearrange("p (k n) -> p k n", k=4)).then_inc(hT_act, 1)

                def attention(m, first):
                    for i in range(2):
                        if not first or i > 0:
                            act.wait_ge(a_sum, m * 2 + i)
                        act.wait_ge(a_picked, m + 1)
                        nc.scalar.activation(an[:, i, :], ap[:, i, :], ACT.Square,
                                             accum_out=ass[:, i:i + 1]).then_inc(a_sum, 1)
                    act.wait_ge(a_sum, m * 2 + 2)
                    if not first:
                        act.wait_ge(a_rs, m)
                    nc.scalar.activation(ars[:], ass[:], ACT.Sqrt, scale=1.0 / 512, bias=t["cols"][:, C_REPS:C_REPS + 1]).then_inc(a_root, 1)
                    for i in range(2):
                        act.wait_ge(a_rs, m + 1)
                        if not first:
                            act.wait_ge(a_turned, m * 2)
                        nc.scalar.activation(an[:, i, :], ap[:, i, :], ACT.Copy, scale=ars[:, i:i + 1]).then_inc(a_norm, 1)

                def step(m, first, last):
                    for i in range(2):
                        act.wait_ge(a_turned, m * 2 + 1 + i)
                        if not first:
                            act.wait_ge(mixed, m * 2 + i - 1)
                        nc.scalar.copy(ah[:, i], A[0][:].rearrange("p (k n) -> p k n", k=4)).then_inc(ah_ready, 1)
                    if not last:
                        attention(m + 1, False)
                    for i in range(2):
                        act.wait_ge(aggr, m * 2 + 1 + i)
                        if not first:
                            act.wait_ge(rstd_ready, m * 2)
                        nc.scalar.activation(sd[:, i:i + 1], mv[:, i, 1:2], ACT.Sqrt, bias=t["cols"][:, C_LEPS:C_LEPS + 1]).then_inc(root, 1)
                        if i == 0 and not first:
                            turned(m * 2 - 1, 1)
                        if not last:
                            split_r(m + 1, i)
                    turned(m * 2, 0)
                split_r(0, 0)
                split_r(0, 1)
                attention(0, True)
                for n, k in enumerate(W_ORDER):
                    act.wait_ge(w_loaded[n % 4], n // 4 * 16 + 16)
                    if k < 4:
                        nc.scalar.activation(wh[:, k], words(n), ACT.Copy, scale=ga[:, k:k + 1]).then_inc(wh_ready, 1)
                    else:
                        nc.scalar.copy(wh[:, k], words(n)).then_inc(wh_ready, 1)
                steps(act, step)
                turned(NT - 1, 1)

            @block.gpsimd
            def _(pool):
                with pool.Fori(0, STEPS) as m:
                    for i in range(2):
                        pool.wait_ge(h_steps, m * 4 + 2 * i + 2)
                        nc.gpsimd.tensor_tensor(hp[:, i], hp[:, i], b1[:], ALU.add).then_inc(h_ready, 1)

            @block.vector
            def _(v):
                hold = Hold("memset", t["cell"], held)

                def turned(n, i):
                    v.wait_ge(h_turned, 2 * n + 1)
                    v.wait_ge(l_done, n)
                    v.tensor_copy(hT[:, i, 0:4, :], H[0][:].rearrange("p (k n) -> p k n", k=4)).then_inc(hT_dve, 1)

                def logged(n):
                    v.wait_ge(l_done, n + 1)
                    v.tensor_tensor(t["lg"][:, bass.ds(n, 1), :], L[:, 0:NG + NE].unsqueeze(1), rb[:].unsqueeze(1), ALU.add).then_inc(l_ready, 1)

                v.wait_ge(c_loaded, 5 * 16)

                def pick(m):
                    if not isinstance(m, int) or m > 0:
                        v.wait_ge(a_norm, m * 2)
                    v.tensor_scalar(ap[:], t["ao"][:, bass.ds(m * 2, 2), :], 1.0, None, ALU.mult).then_inc(a_picked, 1)

                def split_r(m, i):
                    v.wait_ge(rh_ready, m * 2 + i + 1)
                    v.tensor_tensor(rl[:, i], rts[:, :, i * P:(i + 1) * P], rh[:, i].bitcast(F32), ALU.subtract).then_inc(rl_ready, 1)

                def split_a(m, i):
                    v.wait_ge(ah_ready, m * 2 + i + 1)
                    v.tensor_tensor(al[:, i], A[0][:].rearrange("p (k n) -> p k n", k=4), ah[:, i].bitcast(F32),
                                    ALU.subtract).then_inc(al_ready, 1)

                def invert(m):
                    v.wait_ge(a_root, m + 1)
                    v.reciprocal(ars[:], ars[:]).then_inc(a_rs, 1)

                def step(m, first, last):
                    if not last:
                        pick(m + 1)
                    split_a(m, 0)
                    split_a(m, 1)
                    if not last:
                        invert(m + 1)
                    for i in range(2):
                        v.wait_ge(mixed, m * 2 + 1 + i)
                        v.wait_ge(x_loaded, m * 16 + 16)
                        if not first:
                            v.wait_ge(stored[i], m * 16)
                            v.wait_ge(h_turned, m * 4 + 2 * i - 2)
                        for half in range(2):
                            sl = slice(half * 512, (half + 1) * 512)
                            v.scalar_tensor_tensor(hp[:, i, sl], xs[:, i, sl], ALPHA, M[2 * i + half][:], ALU.mult, ALU.add).then_inc(res, 1)
                        for half in range(2):
                            v.wait_ge(res, m * 4 + 2 * i + half + 1)
                            v.bn_stats(st[:, i, half, :], hp[:, i, half * 512:(half + 1) * 512]).then_inc(stats, 1)
                        v.wait_ge(stats, m * 4 + 2 * i + 2)
                        hold(v, m * 2 + i)
                        v.bn_aggr(mv[:, i, :], st[:, i]).then_inc(aggr, 1)
                        v.wait_ge(root, m * 2 + i + 1)
                        v.reciprocal(rstd[:, i:i + 1], sd[:, i:i + 1]).then_inc(rstd_ready, 1)
                        v.wait_ge(rstd_ready, m * 2 + i + 1)
                        v.tensor_scalar(hp[:, i], hp[:, i], mv[:, i, 0:1], rstd[:, i:i + 1], ALU.subtract, ALU.mult).then_inc(h_steps, 1)
                        v.wait_ge(h_steps, m * 4 + 2 * i + 1)
                        v.tensor_tensor(hp[:, i], hp[:, i], g1[:], ALU.mult).then_inc(h_steps, 1)
                        if i == 0 and not first:
                            logged(m * 2 - 2)
                            turned(m * 2 - 1, 1)
                        if not last:
                            split_r(m + 1, i)
                    if not first:
                        logged(m * 2 - 1)
                    turned(m * 2, 0)
                v.wait_ge(c_loaded, 5 * 16)
                v.memset(t["cell"][:, 1:2], 0.0).then_inc(l_ready, 1)
                pick(0)
                split_r(0, 0)
                split_r(0, 1)
                invert(0)
                for n, k in enumerate(W_ORDER):
                    v.wait_ge(wh_ready, n + 1)
                    if k < 4:
                        v.scalar_tensor_tensor(wl[:, k], words(n), ga[:, k:k + 1], wh[:, k].bitcast(F32),
                                               ALU.mult, ALU.subtract).then_inc(wl_ready, 1)
                    else:
                        v.tensor_tensor(wl[:, k], words(n), wh[:, k].bitcast(F32), ALU.subtract).then_inc(wl_ready, 1)
                steps(v, step)
                logged(NT - 2)
                turned(NT - 1, 1)
                logged(NT - 1)


def phase_d(nc, t, d):
    with ExitStack() as ctx:
        sb = lambda name, shape, dt=F32: ctx.enter_context(nc.sbuf_tensor(name, shape, dt))
        sem = lambda name: ctx.enter_context(nc.semaphore(name))
        rows = sb("d_rows", [P, 2 * NE + P])
        before = sb("d_before", [P, P])
        restart = sb("d_restart", [P, NE * NT])
        token = sb("d_token", [P, NT])
        gmax = sb("gmax", [P, NT]); gexp = sb("gexp", [P, NT, NG]); geq = sb("geq", [P, NT, NG])
        gidx = sb("gidx", [P, NT]); pgrp = sb("pgrp", [P, NT])
        e1 = sb("e1", [P, NT, NE]); e2 = sb("e2", [P, NT, NE]); eq = sb("eq", [P, NT, NE])
        m1 = sb("m1", [P, NT]); m2 = sb("m2", [P, NT]); ix = sb("ix", [P, NT]); ee = sb("ee", [P, NT]); de = sb("de", [P, NT])
        oh = sb("oh", [P, 2, NT, NE]); both = sb("both", [P, NT, NE])
        tot = sb("tot", [P, NE, NT]); inc = sb("inc", [P, NE, NT]); rank = sb("rank", [P, NT, NE])
        nblk = sb("nblk", [P, NE]); bend = sb("bend", [P, NE]); bbeg = sb("bbeg", [P, NE])
        blk = sb("blk", [P, NBP, NE]); bex = sb("bex", [P, NBP]); new = sb("new", [P, NBP])
        order = sb("order", [P, NBP + 2]); packed = sb("packed", [P, NBP - 1])
        slot = sb("slot", [P, NT, 2]); bq = sb("bq", [P, NT, 2]); pos = sb("pos", [P, NT, 2])
        at_row = sb("at_row", [P, NT * 2, P]); at_blk = sb("at_blk", [P, NT * 2, NBP])
        wt = ctx.enter_context(nc.psum_tensor("dW", [P, 512], F32))
        al = ctx.enter_context(nc.psum_tensor("dA", [P, 512], F32))
        tk = ctx.enter_context(nc.psum_tensor("dT", [P, 512], F32))
        loaded = sem("d_loaded"); steps = sem("dve_d_steps"); exps = sem("d_exps"); ranks = sem("d_ranks")
        at = {}
        with nc.Block() as block:
            @block.vector
            def _(v):
                n = [0]

                def step(ins, name=None):
                    n[0] += 1
                    ins.then_inc(steps, 1)
                    if name:
                        at[name] = n[0]
                    v.wait_ge(steps, n[0])
                bc = lambda a, k: a.unsqueeze(2).broadcast_to([P, NT, k])
                row = lambda a, b: rows[:, a:b].unsqueeze(1).broadcast_to([P, NT, b - a])
                G, E = t["lg"][:, :, 0:NG], t["lg"][:, :, NG:NG + NE]
                v.wait_ge(loaded, 64)
                step(v.tensor_reduce(gmax[:], G, AX, ALU.max))
                step(v.tensor_tensor(gexp[:], G, bc(gmax[:], NG), ALU.subtract), "gexp")
                step(v.tensor_tensor(geq[:], G, bc(gmax[:], NG), ALU.is_equal))
                step(v.tensor_scalar(geq[:], geq[:], -64.0, 64.0, ALU.mult, ALU.add))
                step(v.tensor_tensor(geq[:], geq[:], row(R_EXPERT, R_EXPERT + NG), ALU.add))
                step(v.tensor_reduce(gidx[:], geq[:], AX, ALU.min))
                step(v.tensor_tensor(eq[:], row(R_GROUP, R_GROUP + NE), bc(gidx[:], NE), ALU.is_equal))
                step(v.tensor_tensor(e1[:], E, eq[:], ALU.mult))
                step(v.tensor_scalar(eq[:], eq[:], BIG, -BIG, ALU.mult, ALU.add))
                step(v.tensor_tensor(e1[:], e1[:], eq[:], ALU.add))
                for k, (src, m) in enumerate(((e1, m1), (e2, m2))):
                    step(v.tensor_reduce(m[:], src[:], AX, ALU.max))
                    step(v.tensor_tensor(eq[:], src[:], bc(m[:], NE), ALU.is_equal))
                    step(v.tensor_scalar(eq[:], eq[:], -64.0, 64.0, ALU.mult, ALU.add))
                    step(v.tensor_tensor(eq[:], eq[:], row(R_EXPERT, R_EXPERT + NE), ALU.add))
                    step(v.tensor_reduce(ix[:], eq[:], AX, ALU.min))
                    step(v.tensor_tensor(oh[:, k], row(R_EXPERT, R_EXPERT + NE), bc(ix[:], NE), ALU.is_equal))
                    if k == 0:
                        step(v.scalar_tensor_tensor(e2[:], oh[:, 0], -BIG, e1[:], ALU.mult, ALU.add))
                step(v.tensor_tensor(both[:], oh[:, 0], oh[:, 1], ALU.add), "both")
                step(v.tensor_tensor(de[:], m2[:], m1[:], ALU.subtract), "de")
                v.wait_ge(exps, 2)
                step(v.tensor_reduce(pgrp[:], gexp[:], AX, ALU.add))
                step(v.tensor_scalar(de[:], ee[:], 1.0, None, ALU.add))
                step(v.tensor_tensor(pgrp[:], pgrp[:], de[:], ALU.mult))
                step(v.reciprocal(pgrp[:], pgrp[:]))
                step(v.tensor_copy(t["gates"][:, :, 0], pgrp[:]))
                step(v.tensor_tensor(t["gates"][:, :, 1], pgrp[:], ee[:], ALU.mult))
                v.wait_ge(ranks, 2)
                step(v.tensor_copy(tot[:], al[:].rearrange("p (n e) -> p e n", e=NE)))
                flat = lambda a: a[:].rearrange("p a b -> p (a b)")
                step(v.tensor_tensor_scan(flat(inc), restart[:], flat(tot), 0.0, ALU.mult, ALU.add))
                step(v.tensor_tensor(tot[:], inc[:], tot[:], ALU.subtract))
                step(v.tensor_scalar(nblk[:], inc[:, :, NT - 1], 1.0 / P, (P - 1.0) / P - 0.49609375, ALU.mult, ALU.add))
                step(v.tensor_scalar(nblk[:], nblk[:], ROUND, None, ALU.add))
                step(v.tensor_scalar(nblk[:], nblk[:], -ROUND, None, ALU.add))
                step(v.tensor_tensor_scan(bend[:], t["ones"][:, 0:NE], nblk[:], 0.0, ALU.mult, ALU.add))
                step(v.tensor_tensor(bbeg[:], bend[:], nblk[:], ALU.subtract))
                step(v.tensor_scalar(bbeg[:], bbeg[:], float(P), None, ALU.mult))
                step(v.tensor_tensor(rank[:], wt[:].rearrange("p (n e) -> p n e", e=NE), tot[:].rearrange("p e n -> p n e"), ALU.add))
                step(v.tensor_tensor(rank[:], rank[:], bbeg[:].unsqueeze(1).broadcast_to([P, NT, NE]), ALU.add))
                for k in range(2):
                    step(v.tensor_tensor(eq[:], oh[:, k], rank[:], ALU.mult))
                    step(v.tensor_reduce(slot[:, :, k], eq[:], AX, ALU.add))
                step(v.tensor_copy(t["slots"][:], slot[:]))
                step(v.tensor_scalar(bq[:], slot[:], 1.0 / P, -0.49609375, ALU.mult, ALU.add))
                step(v.tensor_scalar(bq[:], bq[:], ROUND, None, ALU.add))
                step(v.tensor_scalar(bq[:], bq[:], -ROUND, None, ALU.add))
                step(v.scalar_tensor_tensor(pos[:], bq[:], -float(P), slot[:], ALU.mult, ALU.add))
                pairs = lambda a, w: a.rearrange("p n k -> p (n k)").unsqueeze(2).broadcast_to([P, NT * 2, w])
                count = lambda w: rows[:, R_BLOCK:R_BLOCK + w].unsqueeze(1).broadcast_to([P, NT * 2, w])
                step(v.tensor_tensor(at_row[:], count(P), pairs(pos[:], P), ALU.is_equal))
                step(v.tensor_tensor(at_blk[:], count(NBP), pairs(bq[:], NBP), ALU.is_equal))
                step(v.tensor_tensor(at_blk[:].rearrange("p (n k) b -> p n (k b)", k=2), at_blk[:].rearrange("p (n k) b -> p n (k b)", k=2),
                                     bc(token[:], 2 * NBP), ALU.mult), "at_blk")
                step(v.tensor_tensor(blk[:], bend[:].unsqueeze(1).broadcast_to([P, NBP, NE]),
                                     rows[:, R_BLOCK:R_BLOCK + NBP].unsqueeze(2).broadcast_to([P, NBP, NE]), ALU.is_le))
                step(v.tensor_reduce(bex[:], blk[:], AX, ALU.add))
                step(v.tensor_scalar(bex[:], bex[:], NE - 1.0, None, ALU.min))
                step(v.tensor_copy(t["bexp"][:], bex[:]))
                step(v.tensor_scalar(t["last"][:], bend[:, NE - 1:NE], -1.0, None, ALU.add))
                step(v.tensor_scalar(t["idle"][:], bend[:, NE - 1:NE], -1.0, float(NB), ALU.mult, ALU.add))
                step(v.memset(new[:], 1.0))
                step(v.tensor_tensor(new[:, 1:], bex[:, 1:], bex[:, :NBP - 1], ALU.not_equal))
                step(v.tensor_tensor(bex[:], rows[:, R_BLOCK:R_BLOCK + NBP], bend[:, NE - 1:NE].broadcast_to([P, NBP]), ALU.is_lt))
                step(v.tensor_tensor(new[:], new[:], bex[:], ALU.mult))
                step(v.memset(order[:, 0:2], 0.0))
                step(v.tensor_tensor_scan(order[:, 2:], t["ones"][:, 0:NBP], new[:], 0.0, ALU.mult, ALU.add))
                step(v.tensor_copy(packed[:], order[:, 3:]))
                for back in (2, 1, 0):
                    step(v.scalar_tensor_tensor(packed[:], packed[:], float(FIELD), order[:, back:back + NBP - 1], ALU.mult, ALU.add))
                step(v.tensor_copy(t["ords"][:, 0:NBP - 1], packed[:]))
                v.wait_ge(ranks, 3)
                step(v.tensor_copy(t["tok"][:], tk[:, 0:NBP]))

            @block.scalar
            def _(act):
                act.wait_ge(steps, at["gexp"])
                nc.scalar.activation(gexp[:], gexp[:], ACT.Exp).then_inc(exps, 1)
                act.wait_ge(steps, at["de"])
                nc.scalar.activation(ee[:], de[:], ACT.Exp).then_inc(exps, 1)

            @block.tensor
            def _(pe):
                pe.wait_ge(steps, at["both"])
                b = both[:].rearrange("p n e -> p (n e)")
                pe.matmul(wt[:], before[:], b, start=True, stop=True).then_inc(ranks, 1)
                pe.matmul(al[:], t["ones"][:], b, start=True, stop=True).then_inc(ranks, 1)
                pe.wait_ge(steps, at["at_blk"])
                for n in range(2 * NT):
                    ins = pe.matmul(tk[:, 0:NBP], at_row[:, n], at_blk[:, n], start=(n == 0), stop=(n == 2 * NT - 1))
                ins.then_inc(ranks, 1)

            @block.sync
            def _(sp):
                for dst, src in ((rows, "rows"), (before, "before"), (restart, "restart_tiles"), (token, "token")):
                    sp.dma_start(dst[:], d[src]).then_inc(loaded, 16)

def phase_e(nc, t, d):
    with ExitStack() as ctx:
        sb = lambda name, shape, dt=F32: ctx.enter_context(nc.sbuf_tensor(name, shape, dt))
        sem = lambda name: ctx.enter_context(nc.semaphore(name))
        psum = lambda name, n=512: ctx.enter_context(nc.psum_tensor(name, [P, n], F32))

        class Weights:

            def __init__(self, name, k, n):
                self.src = d[name][0].rearrange("e (k p) n -> e p k n", p=P)
                self.raw = sb(name + "_raw", [P, 2 * k, n], F32R)
                self.hi = sb(name + "_hi", [P, k, n], F32R)
                self.k = k
                self.loaded = sem(name + "_loaded")
                self.hi_ready, self.lo_ready = sem(name + "_hi_ready"), sem(name + "_lo_ready")
                self.used = sem(name + "_used")

            def words(self, o):
                return self.raw[:, bass.ds((o & 1) * self.k, self.k)]
        w1, w3, w2 = Weights("w1", KT, DE), Weights("w3", KT, DE), Weights("w2", DE // P, DM)
        idx = sb("idx", [P, 2], U32)
        xg = sb("xg", [P, 2, DM])
        xh = sb("xh", [P, KT, P], F32R); xl = sb("xl", [P, KT, P], F32R)
        up = sb("up", [P, DE])
        uh = sb("uh", [P, DE // P, P], F32R); ul = sb("ul", [P, DE // P, P], F32R)
        y = sb("y", [P, DM])
        blank = sb("blank", [P, DM])
        X = [psum("eX0"), psum("eX1")]; U = psum("eU"); H1 = psum("eH1"); H3 = psum("eH3"); Y = [psum("eY0"), psum("eY1")]
        idx_ready = sem("idx_ready"); gathered = sem("gathered"); x_turned = sem("xg_turned"); xh_ready = sem("xh_ready"); xl_ready = sem("xl_ready")
        silu = sem("silu_done"); gated = sem("gated"); up_turned = sem("up_turned"); uh_ready = sem("uh_ready"); ul_ready = sem("ul_ready")
        y_dve = sem("y_dve"); y_act = sem("y_act"); stored = sem("y_stored"); held = sem("hold_e"); blanked = sem("blanked"); blanks_stored = sem("blanks_stored")
        yd = d["y"].rearrange("(b p) n -> b p n", p=P)
        def by_side(eng, b, act):
            if isinstance(b, int):
                act(b & 1)
            else:
                for side in range(2):
                    with eng.If((b & 1) == side):
                        act(side)
        four = lambda a: a.rearrange("p (k n) -> p k n", k=4)

        def cell(eng, name, b):
            low, top = {"ords": (0, NE * (FIELD ** 3 + FIELD ** 2 + FIELD + 1)), "bexp": (0, NE - 1), "last": (LEAST - 1, NB - 1), "idle": (0, NB - LEAST)}[name]
            col = t[name][0:1, b:b + 1] if isinstance(b, int) else t[name][0:1, bass.ds(b, 1)]
            return eng.value_load(col, min_val=low, max_val=top)

        class Order:

            def __init__(self, eng, b):
                word = cell(eng, "ords", b)
                field = lambda n: (word >> (6 * n)) & (FIELD - 1)
                self.after, self.here, self.before, self.before2 = (field(n) for n in (3, 2, 1, 0))

        def blocks(eng, stage):
            last = cell(eng, "last", 0)
            stage(0)
            stage(1)
            with eng.Fori(2, NB) as b:
                with eng.If(b <= last):
                    stage(b)
            return last

        def where_new(eng, o, before, act):
            with eng.If(o > before):
                act(o, before)

        with nc.Block() as block:
            @block.sync
            def _(sp):
                def load(w, b, o, before):
                    e = cell(sp, "bexp", b)

                    def fetch(side):
                        if before is not None:
                            sp.wait_ge(w.hi_ready, before)
                        sp.dma_start(w.raw[:, side * w.k:(side + 1) * w.k].bitcast(F32),
                                     w.src[bass.ds(e, 1)].rearrange("o p k n -> p (o k) n")).then_inc(w.loaded, 16)
                    by_side(sp, o, fetch)

                def other(b, o, before, *ws):
                    where_new(sp, o, before, lambda o, before: [load(w, b, o, before) for w in ws])

                def stage(b):
                    if isinstance(b, int) and b == 0:
                        for w in (w1, w3, w2):
                            load(w, 0, 1, None)
                        return
                    order = Order(sp, b)
                    other(b, order.here, order.before, w1, w3)
                    if not isinstance(b, int):
                        other(b - 1, order.before, order.before2, w2)
                    with sp.If(last < NB - b):
                        sp.dma_start(yd[NB - b], blank[:]).then_inc(blanks_stored, 16)
                for name, src in (("g2", "ln2_g"), ("b2", "ln2_b")):
                    sp.dma_start(t[name][:], d[src].broadcast_to([P, DM])).then_inc(t["ln2_loaded"], 16)
                last = cell(sp, "last", 0)
                sp.wait_ge(blanked, 1)
                blocks(sp, stage)
                order = Order(sp, last)
                other(last, order.here, order.before, w2)

            @block.gpsimd
            def _(pool):
                hold = Hold("add", t["cell"], held)

                def gather(b):
                    if not isinstance(b, int) or b > 0:
                        pool.wait_ge(gathered, b * 16)
                    if not isinstance(b, int) or b > 1:
                        pool.wait_ge(x_turned, b * 2 - 2)
                    pool.wait_ge(idx_ready, b + 1)
                    hold(nc.gpsimd, b)

                    def fetch(side):
                        nc.gpsimd.indirect_dma_start(out=xg[:, side], out_offset=None, in_=d["h"],
                                                     in_offset=bass.IndirectOffsetOnAxis(ap=idx[:, side:side + 1], axis=0)).then_inc(gathered, 16)
                    by_side(pool, b, fetch)
                last = blocks(pool, gather)
                gather(last + 1)
                pool.wait_ge(gathered, last * 16 + 32)
                hold(nc.gpsimd, last + 2)
                pool.wait_ge(stored, last * 16 + 16)
                hold(nc.gpsimd, last + 3)
                idle = cell(pool, "idle", 0)
                with pool.If(idle > 0):
                    pool.wait_ge(blanks_stored, idle * 16)
                    hold(nc.gpsimd, last + 4)

            @block.tensor
            def _(pe):
                def turn_x(b):
                    pe.wait_ge(gathered, b * 16 + 16)
                    if not isinstance(b, int) or b > 0:
                        pe.wait_ge(xh_ready, b * 2)
                        pe.wait_ge(xl_ready, b * 2)

                    def turn(side):
                        for k in range(KT):
                            ins = pe.transpose(X[k // 4][:, (k % 4) * P:(k % 4 + 1) * P], xg[:, side, k * P:(k + 1) * P], t["ident"][:])
                            if k % 4 == 3:
                                ins.then_inc(x_turned, 1)
                    by_side(pe, b, turn)

                def first(b, o):
                    for w, H, free in ((w1, H1, silu), (w3, H3, gated)):
                        if not isinstance(b, int) or b > 0:
                            pe.wait_ge(free, b)
                        pe.wait_ge(w.hi_ready, o)
                        if w is w1:
                            pe.wait_ge(xh_ready, b * 2 + 2)
                            pe.wait_ge(xl_ready, b * 2 + 2)
                        for k in range(KT):
                            pe.matmul(H[:], xh[:, k, :], w.hi[:, k, :], start=(k == 0), stop=False)
                            pe.matmul(H[:], xl[:, k, :], w.hi[:, k, :], start=False, stop=False)
                        pe.wait_ge(w.lo_ready, o)
                        lo = w.words(o)
                        for k in range(KT):
                            ins = pe.matmul(H[:], xh[:, k, :], lo[:, k, :], start=False, stop=(k == KT - 1))
                        ins.then_inc(w.used, 1)

                def second(b, o):
                    if not isinstance(b, int) or b > 0:
                        pe.wait_ge(y_dve, b)
                        pe.wait_ge(y_act, b)
                    pe.wait_ge(uh_ready, b + 1)
                    pe.wait_ge(ul_ready, b + 1)
                    pe.wait_ge(w2.hi_ready, o)
                    K2 = DE // P
                    for half in range(2):
                        at = slice(half * 512, (half + 1) * 512)
                        for k in range(K2):
                            pe.matmul(Y[half][:], uh[:, k, :], w2.hi[:, k, at], start=(k == 0), stop=False)
                            pe.matmul(Y[half][:], ul[:, k, :], w2.hi[:, k, at], start=False, stop=False)
                    pe.wait_ge(w2.lo_ready, o)
                    lo = w2.words(o)
                    for half in range(2):
                        at = slice(half * 512, (half + 1) * 512)
                        for k in range(K2):
                            ins = pe.matmul(Y[half][:], uh[:, k, :], lo[:, k, at], start=False, stop=(k == K2 - 1))
                    ins.then_inc(w2.used, 1)

                def turn_up(b):
                    pe.wait_ge(gated, b + 1)
                    for k in range(DE // P):
                        ins = pe.transpose(U[:, k * P:(k + 1) * P], up[:, k * P:(k + 1) * P], t["ident"][:])
                    ins.then_inc(up_turned, 1)

                def stage(b):
                    order = Order(pe, b)
                    first(b, order.here)
                    turn_x(b + 1)
                    if not isinstance(b, int) or b > 0:
                        second(b - 1, order.before)
                    turn_up(b)
                turn_x(0)
                last = blocks(pe, stage)
                second(last, Order(pe, last).here)

            def split_hi(act, w, b, o=1, before=0):
                def split(o, before):
                    act.wait_ge(w.loaded, o * 16)
                    if not isinstance(b, int) or b > 0:
                        act.wait_ge(w.used, b)
                    nc.scalar.copy(w.hi[:], w.words(o).bitcast(F32)).then_inc(w.hi_ready, 1)
                if isinstance(o, int):
                    split(o, before)
                else:
                    where_new(act, o, before, split)

            def split_lo(v, w, b, o=1, before=0):
                def split(o, before):
                    v.wait_ge(w.hi_ready, o)
                    v.tensor_tensor(w.words(o), w.words(o).bitcast(F32), w.hi[:].bitcast(F32), ALU.subtract).then_inc(w.lo_ready, 1)
                if isinstance(o, int):
                    split(o, before)
                else:
                    where_new(v, o, before, split)

            @block.scalar
            def _(act):
                def x_part(b):
                    for n in range(2):
                        act.wait_ge(x_turned, b * 2 + 1 + n)
                        if not isinstance(b, int) or b > 0:
                            act.wait_ge(w3.used, b)
                        nc.scalar.copy(xh[:, 4 * n:4 * n + 4, :], four(X[n][:])).then_inc(xh_ready, 1)

                def y_part(b):
                    act.wait_ge(w2.used, b + 1)
                    if not isinstance(b, int) or b > 0:
                        act.wait_ge(stored, b * 16)
                    nc.scalar.copy(y[:, 512:], Y[1][:]).then_inc(y_act, 1)
                    act.wait_ge(y_dve, b + 1)
                    act.wait_ge(y_act, b + 1)
                    act.dma_start(yd[b], y[:]).then_inc(stored, 16)

                def stage(b):
                    later = not isinstance(b, int) or b > 0
                    order = Order(act, b)
                    act.wait_ge(w1.used, b + 1)
                    if later:
                        act.wait_ge(up_turned, b)
                    nc.scalar.activation(up[:], H1[:], ACT.Silu).then_inc(silu, 1)
                    if later:
                        split_hi(act, w2, b - 1, order.before, order.before2)
                    split_hi(act, w1, b + 1, order.after, order.here)
                    x_part(b + 1)
                    split_hi(act, w3, b + 1, order.after, order.here)
                    if later:
                        y_part(b - 1)
                    act.wait_ge(up_turned, b + 1)
                    if later:
                        act.wait_ge(w2.used, b)
                    nc.scalar.copy(uh[:], four(U[:])).then_inc(uh_ready, 1)
                split_hi(act, w1, 0)
                x_part(0)
                split_hi(act, w3, 0)
                last = blocks(act, stage)
                order = Order(act, last)
                split_hi(act, w2, last, order.here, order.before)
                y_part(last)

            @block.vector
            def _(v):
                def index(b):
                    if not isinstance(b, int) or b > 1:
                        v.wait_ge(gathered, b * 16 - 16)
                    v.tensor_scalar(idx[:, bass.ds(b & 1, 1)], t["tok"][:, bass.ds(b, 1)], 0.0, None, ALU.add).then_inc(idx_ready, 1)

                def x_part(b):
                    for n in range(2):
                        v.wait_ge(xh_ready, b * 2 + 1 + n)
                        v.tensor_tensor(xl[:, 4 * n:4 * n + 4, :], four(X[n][:]), xh[:, 4 * n:4 * n + 4, :].bitcast(F32),
                                        ALU.subtract).then_inc(xl_ready, 1)

                def y_part(b):
                    v.wait_ge(w2.used, b + 1)
                    if not isinstance(b, int) or b > 0:
                        v.wait_ge(stored, b * 16)
                    v.tensor_copy(y[:, 0:512], Y[0][:]).then_inc(y_dve, 1)

                def stage(b):
                    later = not isinstance(b, int) or b > 0
                    order = Order(v, b)
                    index(b + 2)
                    if later:
                        split_lo(v, w2, b - 1, order.before, order.before2)
                    v.wait_ge(silu, b + 1)
                    v.wait_ge(w3.used, b + 1)
                    v.tensor_tensor(up[:], up[:], H3[:], ALU.mult).then_inc(gated, 1)
                    x_part(b + 1)
                    split_lo(v, w1, b + 1, order.after, order.here)
                    if later:
                        y_part(b - 1)
                    v.wait_ge(uh_ready, b + 1)
                    v.tensor_tensor(ul[:], four(U[:]), uh[:].bitcast(F32), ALU.subtract).then_inc(ul_ready, 1)
                    split_lo(v, w3, b + 1, order.after, order.here)
                v.memset(blank[:], 0.0).then_inc(blanked, 1)
                index(0)
                index(1)
                split_lo(v, w1, 0)
                x_part(0)
                split_lo(v, w3, 0)
                last = blocks(v, stage)
                order = Order(v, last)
                split_lo(v, w2, last, order.here, order.before)
                y_part(last)


def phase_f(nc, t, d):
    TS = 4
    with ExitStack() as ctx:
        sb = lambda name, shape, dt=F32: ctx.enter_context(nc.sbuf_tensor(name, shape, dt))
        sem = lambda name: ctx.enter_context(nc.semaphore(name))
        g2, b2, loaded = t["g2"], t["b2"], t["ln2_loaded"]
        idx = sb("fidx", [P, TS, 2], U32); gt = sb("fgt", [P, TS, 2])
        yg = sb("yg", [P, TS, 2, DM])
        hs = sb("fhs", [P, TS, DM])
        z = sb("fz", [P, TS, DM])
        st = sb("fst", [P, TS, 2, 6]); mv = sb("fmv", [P, TS, 2]); sd = sb("fsd", [P, TS]); rstd = sb("frstd", [P, TS]); nmr = sb("fnmr", [P, TS])
        idx_ready = sem("f_idx"); gt_ready = sem("f_gt"); got = [sem(f"f_got{i}") for i in range(TS)]
        h_loaded = [sem(f"f_h{i}") for i in range(TS)]; first = sem("f_first"); second = sem("f_second"); stats = sem("f_stats"); aggr = sem("f_aggr")
        root = sem("f_root"); factored = sem("f_factored"); normed = sem("f_normed"); scaled = sem("f_scaled"); done = sem("f_done"); stored = [sem(f"f_stored{i}") for i in range(TS)]
        held = sem("hold_f"); held_v = sem("hold_fv")
        hd = d["h"].rearrange("(m i p) n -> m i p n", i=TS, p=P)
        od = d["out"][0].rearrange("(m i p) n -> m i p n", i=TS, p=P)
        M = NT // TS

        def steps(eng, step):
            step(0)
            with eng.Fori(1, M - 1) as m:
                step(m)
            step(M - 1)

        is_first = lambda m: isinstance(m, int) and m == 0
        is_last = lambda m: isinstance(m, int) and m == M - 1

        with nc.Block() as block:
            @block.sync
            def _(sp):
                for i in range(TS):
                    if i > 0:
                        sp.wait_ge(got[i - 1], 32)
                    sp.dma_start(hs[:, i], hd[0, i]).then_inc(h_loaded[i], 16)

                def step(m):
                    for i in range(TS):
                        if not is_last(m):
                            sp.wait_ge(second, (m * TS + i) * 2 + 2)
                            sp.dma_start(hs[:, i], hd[m + 1, i]).then_inc(h_loaded[i], 16)
                        if i >= 2 or not is_first(m):
                            store(m, i - 2)

                def store(m, i):
                    sp.wait_ge(done, m * TS + i + 1)
                    sp.dma_start(od[m, i] if i >= 0 else od[m - 1, i + TS], z[:, i % TS]).then_inc(stored[i % TS], 16)
                steps(sp, step)
                store(M - 1, TS - 2)
                store(M - 1, TS - 1)
                for i in range(TS):
                    sp.wait_ge(stored[i], 16 * M)

            @block.gpsimd
            def _(pool):
                hold = Hold("add", t["cell"], held)

                def gather(m, i):
                    pool.wait_ge(idx_ready, m + 1)
                    if not is_first(m):
                        pool.wait_ge(second, (m * TS + i) * 2 - (TS * 2 - 2))
                    hold(nc.gpsimd, m * TS + i)
                    for k in range(2):
                        nc.gpsimd.indirect_dma_start(out=yg[:, i, k], out_offset=None, in_=d["y"],
                                                     in_offset=bass.IndirectOffsetOnAxis(ap=idx[:, i, k:k + 1], axis=0)).then_inc(got[i], 16)

                def shift(m, i):
                    pool.wait_ge(scaled, m * TS + i + 1)
                    nc.gpsimd.tensor_tensor(z[:, i % TS], z[:, i % TS], b2[:], ALU.add).then_inc(done, 1)

                def step(m):
                    for i in range(TS):
                        if i == TS - 1 and not is_last(m):
                            for j in range(TS - 1):
                                gather(m + 1, j)
                        if i >= 2 or not is_first(m):
                            shift(m, i - 2)
                    if not is_last(m):
                        gather(m + 1, TS - 1)
                for i in range(TS):
                    gather(0, i)
                pool.wait_ge(loaded, 32)
                steps(pool, step)
                shift(M - 1, TS - 2)
                shift(M - 1, TS - 1)

            @block.scalar
            def _(act):
                def weigh(m, i):
                    act.wait_ge(gt_ready, m + 1)
                    act.wait_ge(got[i], m * 32 + 32)
                    nc.scalar.activation(yg[:, i, 0], yg[:, i, 0], ACT.Copy, scale=gt[:, i, 0:1]).then_inc(first, 1)

                def take_root(m, i):
                    j = i % TS
                    act.wait_ge(aggr, m * TS + i + 1)
                    nc.scalar.activation(sd[:, j:j + 1], mv[:, j, 1:2], ACT.Sqrt, bias=t["cols"][:, C_LEPS:C_LEPS + 1]).then_inc(root, 1)

                def norm(m, i):
                    j = i % TS
                    act.wait_ge(factored, (m * TS + i) * 2 + 2)
                    nc.scalar.activation(z[:, j], z[:, j], ACT.Identity, scale=rstd[:, j:j + 1],
                                         bias=nmr[:, j:j + 1]).then_inc(normed, 1)

                def step(m):
                    for i in range(TS):
                        earlier = i >= 1 or not is_first(m)
                        if earlier:
                            take_root(m, i - 1)
                        if i < TS - 1:
                            weigh(m, i + 1)
                        elif not is_last(m):
                            weigh(m + 1, 0)
                        if earlier:
                            norm(m, i - 1)
                weigh(0, 0)
                steps(act, step)
                take_root(M - 1, TS - 1)
                norm(M - 1, TS - 1)

            @block.vector
            def _(v):
                hold = Hold("memset", t["cell"], held_v)

                def pick_slots(m):
                    v.tensor_scalar(idx[:], t["slots"][:, bass.ds(m * TS, TS), :], 0.0, None, ALU.add).then_inc(idx_ready, 1)

                def pick_gates(m):
                    v.tensor_scalar(gt[:], t["gates"][:, bass.ds(m * TS, TS), :], 1.0, None, ALU.mult).then_inc(gt_ready, 1)

                def combine(m, i):
                    n = m * TS + i
                    refill = i == TS - 1 and not is_last(m)
                    if refill:
                        for j in range(TS):
                            v.wait_ge(got[j], m * 32 + 32)
                        pick_slots(m + 1)
                    if i == 0:
                        v.wait_ge(gt_ready, m + 1)
                    v.wait_ge(first, n + 1)
                    v.scalar_tensor_tensor(yg[:, i, 1], yg[:, i, 1], gt[:, i, 1:2], yg[:, i, 0], ALU.mult, ALU.add).then_inc(second, 1)
                    v.wait_ge(second, n * 2 + 1)
                    if refill:
                        pick_gates(m + 1)
                    v.wait_ge(h_loaded[i], m * 16 + 16)
                    if not is_first(m):
                        v.wait_ge(stored[i], m * 16)
                    v.scalar_tensor_tensor(z[:, i], hs[:, i], ALPHA, yg[:, i, 1], ALU.mult, ALU.add).then_inc(second, 1)
                    v.wait_ge(second, n * 2 + 2)
                    for half in range(2):
                        v.bn_stats(st[:, i, half], z[:, i, half * 512:(half + 1) * 512]).then_inc(stats, 1)
                    v.wait_ge(stats, n * 2 + 2)
                    hold(v, n)
                    v.bn_aggr(mv[:, i], st[:, i]).then_inc(aggr, 1)

                def factors(m, i):
                    n, j = m * TS + i, i % TS
                    v.wait_ge(root, n + 1)
                    v.reciprocal(rstd[:, j:j + 1], sd[:, j:j + 1]).then_inc(factored, 1)
                    v.wait_ge(factored, n * 2 + 1)
                    v.scalar_tensor_tensor(nmr[:, j:j + 1], mv[:, j, 0:1], -1.0, rstd[:, j:j + 1], ALU.mult, ALU.mult).then_inc(factored, 1)

                def gain(m, i):
                    v.wait_ge(normed, m * TS + i + 1)
                    v.tensor_tensor(z[:, i % TS], z[:, i % TS], g2[:], ALU.mult).then_inc(scaled, 1)

                def step(m):
                    for i in range(TS):
                        combine(m, i)
                        if i >= 1 or not is_first(m):
                            factors(m, i - 1)
                        if i >= 2 or not is_first(m):
                            gain(m, i - 2)
                pick_slots(0)
                pick_gates(0)
                v.wait_ge(loaded, 32)
                steps(v, step)
                factors(M - 1, TS - 1)
                gain(M - 1, TS - 2)
                gain(M - 1, TS - 1)


def build(nc, d):
    with ExitStack() as ctx:
        t = {}

        def keep(ctx, name, shape, dt=F32):
            t[name] = ctx.enter_context(nc.sbuf_tensor(name, shape, dt))
        for name in ("ident", "fold", "causal", "ones"):
            keep(ctx, name, [P, P])
        keep(ctx, "cols", [P, 8])
        keep(ctx, "cell", [P, 8])
        keep(ctx, "lg", [P, NT, NG + NE])
        t["w_in_loaded"] = [ctx.enter_context(nc.semaphore(f"w_in_loaded{i}")) for i in range(len(W_PARTS))]
        t["x_loaded"] = ctx.enter_context(nc.semaphore("x_loaded"))
        with ExitStack() as attn:
            keep(attn, "trig", [P, SEQ])
            keep(attn, "cqn", [P, 2, SEQ])
            keep(attn, "ckvn", [P, SEQ])
            keep(attn, "krp", [P, SEQ])
            for name, n in (("gq", 2), ("gkv", 1)):
                keep(attn, name, [P, n])
            with ExitStack() as proj:
                keep(proj, "wi", [P, KT, W_COLS])
                keep(proj, "restart", [P, HG * SPAN])
                keep(proj, "xt", [P, 2, DM])
                for name, n in (("ghg", 1), ("lb", HG), ("oml", HG), ("noml", HG)):
                    keep(proj, name, [P, n])
                phase_0(nc, t, d)
                phase_a(nc, t, d)
            keep(attn, "ao", [P, NT, HEADS * VD])
            for name, shape in (("wr", [P, KT, NG + NE]), ("rb", [P, NG + NE]), ("ga", [P, 4]),
                                ("g1", [P, DM]), ("b1", [P, DM])):
                keep(attn, name, shape)
            t["c_loaded"] = attn.enter_context(nc.semaphore("c_loaded"))
            phase_b(nc, t, d)
            phase_c(nc, t, d)
        route_and_experts(nc, t, d)


def route_and_experts(nc, t, d):
    with ExitStack() as ctx:
        for name, shape, dt in (("gates", [P, NT, 2], F32), ("slots", [P, NT, 2], U32),
                                ("tok", [P, NBP], I32), ("bexp", [P, NBP], I32), ("ords", [P, NBP], I32),
                                ("last", [P, 1], I32), ("idle", [P, 1], I32)):
            t[name] = ctx.enter_context(nc.sbuf_tensor(name, shape, dt))
        for name in ("g2", "b2"):
            t[name] = ctx.enter_context(nc.sbuf_tensor(name, [P, DM], F32))
        t["ln2_loaded"] = ctx.enter_context(nc.semaphore("ln2_loaded"))
        phase_d(nc, t, d)
        phase_e(nc, t, d)
        phase_f(nc, t, d)


INPUTS = ("x", "positions", "w_in", "q_norm_g", "w_uq", "kv_norm_g", "w_ukv", "mla_out_g", "hg_lb_logits", "hg_norm_g",
          "w_out", "ln1_g", "ln1_b", "w_router", "b_router", "w1", "w3", "w2", "ln2_g", "ln2_b")
SCRATCH = (("rT", (D_HG, SEQ), F32), ("h", (SEQ, DM), F32), ("y", (NB * P, DM), F32))


def kernel(**inputs):
    import concourse.bacc as bacc
    from concourse.bass_utils import run_bass_kernel_spmd as run

    laid = lay_out(inputs)
    arrays = {n: laid[n] for n in INPUTS}
    arrays.update(shape_constants())
    arrays = {"in_" + n: np.ascontiguousarray(a) for n, a in arrays.items()}
    nc = bacc.Bacc("TRN2", target_bir_lowering=False, num_devices=1)
    d = {n[3:]: nc.dram_tensor(n, a.shape, mybir.dt.from_np(a.dtype), kind="ExternalInput").ap() for n, a in arrays.items()}
    for name, shape, dt in SCRATCH:
        d[name] = nc.dram_tensor("scratch_" + name, shape, dt, kind="Internal").ap()
    d["out"] = nc.dram_tensor("out", (1, SEQ, DM), F32, kind="ExternalOutput").ap()
    build(nc, d)
    r = run(nc, [arrays], core_ids=[0])
    return r.results[0]["out"]
```
